# Optimizing a Trainium2 kernel written in Bass

```python
import math
import jax, jax.numpy as jnp
from jax import lax
import numpy as np

D_MODEL = 1024
BATCH = 1
SEQ = 512
DEPTH = 2

CHUNK = 64
MIX_WIDTH = D_MODEL
GMLP_WIDTH = MIX_WIDTH // 2
GMLP_GROUPS = 4
GMLP_GROUP_DIM = GMLP_WIDTH // GMLP_GROUPS
GMLP_BLOCK = 128
DIFF_WIDTH = MIX_WIDTH - GMLP_WIDTH
DIFF_HEADS = 4
DIFF_VDIM = DIFF_WIDTH // DIFF_HEADS
DIFF_QK_DIM = DIFF_VDIM // 2
ROPE_THETA = 10000.0
QBLK = 128
FFN_HIDDEN = int(math.ceil(8 * D_MODEL / 3 / 256)) * 256
Q_WIDTH = DIFF_HEADS * 2 * DIFF_QK_DIM
K_WIDTH = DIFF_HEADS * 2 * DIFF_QK_DIM
IN_WIDTH = 2 * GMLP_WIDTH + Q_WIDTH + K_WIDTH + DIFF_WIDTH
NORM_EPS = 1e-6
NEG_INF = -1e30

kernel_name = "hybrid_gmlp_diffattn_sandwich"

def rms_norm(x, g, eps=NORM_EPS):
    xf = x.astype(jnp.float32)
    y = xf * lax.rsqrt(jnp.mean(xf * xf, axis=-1, keepdims=True) + eps)
    return (y * g.astype(jnp.float32)).astype(x.dtype)

def layer_norm(x, g, b, eps=NORM_EPS):
    xf = x.astype(jnp.float32)
    mu = jnp.mean(xf, axis=-1, keepdims=True)
    xc = xf - mu
    y = xc * lax.rsqrt(jnp.mean(xc * xc, axis=-1, keepdims=True) + eps)
    return (y * g.astype(jnp.float32) + b.astype(jnp.float32)).astype(x.dtype)

def rope_tables(seq, dim):
    inv = 1.0 / (ROPE_THETA ** (jnp.arange(0, dim, 2, dtype=jnp.float32) / dim))
    ang = jnp.arange(seq, dtype=jnp.float32)[:, None] * inv[None, :]
    return jnp.cos(ang), jnp.sin(ang)

def apply_rope(x, cos, sin):
    xf = x.astype(jnp.float32)
    half = xf.shape[-1] // 2
    x1, x2 = xf[..., :half], xf[..., half:]
    c = cos[:, None, None, :]
    s = sin[:, None, None, :]
    return jnp.concatenate([x1 * c - x2 * s, x2 * c + x1 * s], axis=-1).astype(x.dtype)

def gmlp_mixer(u, v, ln_g, ln_b, ws, bias):
    bsz, seq, _ = u.shape
    n = seq // GMLP_BLOCK
    v = layer_norm(v, ln_g, ln_b)
    v = v.reshape(bsz, n, GMLP_BLOCK, GMLP_GROUPS, GMLP_GROUP_DIM)
    t_chunk = jnp.arange(GMLP_BLOCK) // CHUNK
    mask = t_chunk[None, :] <= t_chunk[:, None]
    w = jnp.where(mask[None], ws, jnp.zeros_like(ws)).astype(v.dtype)
    mixed = jnp.einsum('gts,bnsgc->bntgc', w, v)
    mixed = mixed + jnp.transpose(bias)[:, :, None].astype(v.dtype)
    out = u.reshape(bsz, n, GMLP_BLOCK, GMLP_GROUPS, GMLP_GROUP_DIM) * mixed
    return out.reshape(bsz, seq, GMLP_WIDTH)

def diff_attention(q, k, v, cos, sin, lam, lam_init, subln_g):
    bsz, seq, _ = q.shape
    q = q.reshape(bsz, seq, DIFF_HEADS, 2, DIFF_QK_DIM)
    k = k.reshape(bsz, seq, DIFF_HEADS, 2, DIFF_QK_DIM)
    v = v.reshape(bsz, seq, DIFF_HEADS, DIFF_VDIM)
    q = apply_rope(q, cos, sin) * (DIFF_QK_DIM ** -0.5)
    k = apply_rope(k, cos, sin)
    k_chunk = jnp.arange(seq) // CHUNK
    n_blk = seq // QBLK

    def block(i):
        qb = lax.dynamic_slice_in_dim(q, i * QBLK, QBLK, axis=1)
        s = jnp.einsum('bqhjd,bkhjd->jbhqk', qb, k).astype(jnp.float32)
        q_chunk = (i * QBLK + jnp.arange(QBLK)) // CHUNK
        mask = k_chunk[None, :] <= q_chunk[:, None]
        s = jnp.where(mask, s, NEG_INF)
        p = jax.nn.softmax(s, axis=-1)
        a = p[0] - lam * p[1]
        return jnp.einsum('bhqk,bkhe->bqhe', a.astype(v.dtype), v)

    o = lax.map(block, jnp.arange(n_blk))
    o = jnp.transpose(o, (1, 0, 2, 3, 4)).reshape(bsz, seq, DIFF_HEADS, DIFF_VDIM)
    o = rms_norm(o, subln_g) * (1.0 - lam_init)
    return o.reshape(bsz, seq, DIFF_WIDTH).astype(q.dtype)

def setup_inputs(seed: int = 0) -> dict:
    key = jax.random.key(seed)
    ks = jax.random.split(key, 24)
    f32 = jnp.float32
    nrm = lambda k, shape, scale: jax.random.normal(k, shape, f32) * scale
    gain = lambda k, shape: 1.0 + 0.05 * jax.random.normal(k, shape, f32)
    return {
        "x": jax.random.normal(ks[0], (BATCH, SEQ, D_MODEL), f32),
        "pre_mix_g": gain(ks[1], (DEPTH, D_MODEL)),
        "w_in": nrm(ks[2], (DEPTH, D_MODEL, IN_WIDTH), D_MODEL ** -0.5),
        "gmlp_ln_g": gain(ks[3], (DEPTH, GMLP_WIDTH)),
        "gmlp_ln_b": nrm(ks[4], (DEPTH, GMLP_WIDTH), 0.02),
        "gmlp_ws": nrm(ks[5], (DEPTH, GMLP_GROUPS, GMLP_BLOCK, GMLP_BLOCK), GMLP_BLOCK ** -0.5),
        "gmlp_b": gain(ks[6], (DEPTH, GMLP_GROUPS, GMLP_BLOCK)),
        "lambda_q1": nrm(ks[7], (DEPTH, DIFF_QK_DIM), 0.1),
        "lambda_k1": nrm(ks[8], (DEPTH, DIFF_QK_DIM), 0.1),
        "lambda_q2": nrm(ks[9], (DEPTH, DIFF_QK_DIM), 0.1),
        "lambda_k2": nrm(ks[10], (DEPTH, DIFF_QK_DIM), 0.1),
        "subln_g": gain(ks[11], (DEPTH, DIFF_VDIM)),
        "w_out": nrm(ks[12], (DEPTH, MIX_WIDTH, D_MODEL), MIX_WIDTH ** -0.5),
        "post_mix_g": gain(ks[13], (DEPTH, D_MODEL)),
        "pre_ffn_g": gain(ks[14], (DEPTH, D_MODEL)),
        "w_gate_up": nrm(ks[15], (DEPTH, D_MODEL, 2 * FFN_HIDDEN), D_MODEL ** -0.5),
        "w_down": nrm(ks[16], (DEPTH, FFN_HIDDEN, D_MODEL), FFN_HIDDEN ** -0.5),
        "post_ffn_g": gain(ks[17], (DEPTH, D_MODEL)),
    }

def reference(x, pre_mix_g, w_in, gmlp_ln_g, gmlp_ln_b, gmlp_ws, gmlp_b,
              lambda_q1, lambda_k1, lambda_q2, lambda_k2, subln_g, w_out,
              post_mix_g, pre_ffn_g, w_gate_up, w_down, post_ffn_g):
    seq = x.shape[1]
    cos, sin = rope_tables(seq, DIFF_QK_DIM)
    o_u = 0
    o_v = GMLP_WIDTH
    o_q = 2 * GMLP_WIDTH
    o_k = o_q + Q_WIDTH
    o_val = o_k + K_WIDTH
    for l in range(DEPTH):
        h = rms_norm(x, pre_mix_g[l])
        z = jnp.einsum('bsd,de->bse', h, w_in[l])
        uv = jax.nn.gelu(z[..., o_u:o_q], approximate=False)
        u, v_g = uv[..., :GMLP_WIDTH], uv[..., GMLP_WIDTH:]
        y_a = gmlp_mixer(u, v_g, gmlp_ln_g[l], gmlp_ln_b[l], gmlp_ws[l], gmlp_b[l])

        lam_init = 0.8 - 0.6 * math.exp(-0.3 * l)
        lam = (jnp.exp(jnp.sum(lambda_q1[l].astype(jnp.float32) * lambda_k1[l].astype(jnp.float32)))
               - jnp.exp(jnp.sum(lambda_q2[l].astype(jnp.float32) * lambda_k2[l].astype(jnp.float32)))
               + lam_init)
        y_b = diff_attention(z[..., o_q:o_k], z[..., o_k:o_val], z[..., o_val:],
                             cos, sin, lam, lam_init, subln_g[l])

        mix = jnp.einsum('bse,ed->bsd', jnp.concatenate([y_a, y_b], axis=-1), w_out[l])
        x = x + rms_norm(mix, post_mix_g[l])

        h = rms_norm(x, pre_ffn_g[l])
        gu = jnp.einsum('bsd,df->bsf', h, w_gate_up[l])
        gate, up = gu[..., :FFN_HIDDEN], gu[..., FFN_HIDDEN:]
        y = jnp.einsum('bsf,fd->bsd', jax.nn.silu(gate) * up, w_down[l])
        x = x + rms_norm(y, post_ffn_g[l])
    return x


_drawn_inputs = setup_inputs


def setup_inputs(seed=0):
    import zlib

    import numpy as np

    out = dict(_drawn_inputs(seed))
    spreads = {}
    factors = {'gmlp_ln_b': 5.784, 'lambda_q2': 3.848}
    for name, (base, spread) in spreads.items():
        noise = np.random.default_rng([zlib.crc32(name.encode()), seed]).standard_normal(out[name].shape)
        drawn = base * np.exp(spread * noise) if base else spread * noise
        out[name] = __import__('jax').numpy.asarray(drawn.astype(out[name].dtype))
    for name, factor in factors.items():
        out[name] = (out[name] * factor).astype(out[name].dtype)
    return out
```

```python
import math
from contextlib import ExitStack

import numpy as np

import concourse.bass as bass
from concourse import mybir

F32 = mybir.dt.float32
F32R = mybir.dt.float32r
ALU = mybir.AluOpType
ACT = mybir.ActivationFunctionType
AX_X = mybir.AxisListType.X

P = 128
EPS = 1e-6
NEG_INF = -1e30


def at(l, n, k):
    return l * n + k


def trunk(nc, x, pre_mix_g, w_in, gmlp_ln_g, gmlp_ln_b, gmlp_ws, gmlp_b, lambda_q1, lambda_k1, lambda_q2,
          lambda_k2, subln_g, w_out, post_mix_g, pre_ffn_g, w_gate_up, w_down, post_ffn_g, rope, out):
    L, D, IN = w_in.shape
    S = x.shape[1]
    FF = w_down.shape[1]
    KT = D // P
    ST = S // P
    G = gmlp_ws.shape[1]
    H = G
    HD = lambda_q1.shape[1]
    CH = 64
    FT = FF // P
    FH = FT // 2
    SCALE = HD ** -0.5
    U0, V0, Q0, K0, A0 = 0, G * P, 2 * G * P, 3 * G * P, 4 * G * P
    assert L == 2 and (S, ST, KT, IN) == (512, 4, 2 * G, 5 * G * P) and 2 * HD == P and FT % 2 == 0

    C_QK, C_VG, C_VA, C_U, C_OUT, C_GU = 0, 4, 6, 8, 10, 14
    C_DOWN = C_GU + FT
    NC = C_DOWN + 2 * KT
    CE = KT * 2 * P
    CD = FH * P
    assert NC % 2 == 0
    QK_TILES = [(K0, 0), (K0, 1), (Q0, 0), (Q0, 1), (K0, 2), (K0, 3), (Q0, 2), (Q0, 3)]
    QK_BANKS = [0, 1, 2, 3, 5, 6, 0, 1]

    POST_MIX, PRE_FFN, POST_FFN, NEXT_MIX, LN_G, LN_B, SUBLN, NEG_LAM = 0, 8, 16, 24, 32, 36, 40, 41
    NPAR = 42
    PAR_ROWS = L * NEG_LAM + KT
    NS = H * ST
    TABLES = 3
    PAR_DMAS = 7 * L + 1
    PAR_STEPS = 2 + 2 * L
    LAM_INIT = [0.8 - 0.6 * math.exp(-0.3 * l) for l in range(L)]

    ctx = ExitStack()
    with ctx:
        def sb(name, shape, dt=F32, stack=ctx):
            return stack.enter_context(nc.sbuf_tensor(name, shape, dt))

        def sem(name):
            return ctx.enter_context(nc.semaphore(name))

        xT = sb("xT", [P, KT, S])
        yT = sb("yT", [P, KT, S])
        xg_hi = sb("xg_hi", [P, KT, S], F32R)
        xg_lo = sb("xg_lo", [P, KT, S], F32R)
        raw = sb("raw", [P, 2, CE])
        w_hi = sb("w_hi", [P, 2, 2, CE // 2], F32R)
        w_lo = sb("w_lo", [P, 2, 2, CE // 2], F32R)
        rstd_x = sb("rstd_x", [P, S])
        sq_sum = sb("sq_sum", [P, S])
        diag = sb("diag", [P, ST, P])
        ident = sb("ident", [P, P])
        ones = sb("ones", [P, P])
        par_all = sb("par_all", [P, L, NPAR])
        par = sb("par", [P, NPAR])
        gain0 = sb("gain0", [P, KT])
        eps = sb("eps", [P, 1])
        root = sb("root", [P, ST])
        rcol = sb("rcol", [P, 2, ST])
        taken = [0]

        def small(*shape):
            n = math.prod(shape)
            t = sq_sum[:, taken[0]:taken[0] + n]
            taken[0] += n
            names = "abc"[:len(shape)]
            return t.rearrange(f"p ({' '.join(names)}) -> p {' '.join(names)}", **dict(zip(names, shape)))

        mx = small(2)
        nmx = small(2, 2)
        psumr = small(2, 2)
        rinv = small(2)
        w1 = small(1)
        lam_sum = small(2, L)
        lam_exp = small(2, L)
        lam_d = small(L)
        stats = small(ST, 6)
        mv = small(ST, 2)
        ln_root = small(ST)
        ln_rs = small(ST)
        o_mean = small(H, ST)
        o_root = small(H, ST)
        o_rs = small(H, ST)
        with ExitStack() as mixers:
            q_rot = sb("q_rot", [P, H, S], stack=mixers)
            k_rot = sb("k_rot", [P, H, S], stack=mixers)
            swap = sb("swap", [P, 2, S], stack=mixers)
            v_att = sb("v_att", [P, ST, H * P], stack=mixers)
            v_gate = sb("v_gate", [P, ST, G * P], stack=mixers)
            prob = sb("prob", [P, 2, 2, S], stack=mixers)
            attn = sb("attn", [P, 2, S], stack=mixers)
            attnT = sb("attnT", [P, 2, ST, S], stack=mixers)
            o_sq = sb("o_sq", [P, S], stack=mixers)
            trig = sb("trig", [P, 2, S], stack=mixers)
            ws = sb("ws", [P, G, P], stack=mixers)
            wsT = sb("wsT", [P, G, P], stack=mixers)
            g_bias = sb("g_bias", [P, G, P], stack=mixers)
            add_t = sb("add_t", [P, G, P], stack=mixers)
        hid_hi = sb("hid_hi", [P, FT, S], F32R)
        hid_lo = sb("hid_lo", [P, FT, S], F32R)
        oT = yT[:, 0:H, :]
        uT = yT[:, H:H + G, :]
        gate_t = yT[:, 0:2, :]
        up_t = yT[:, 2:4, :]
        rows = attnT[:, :, :, :].rearrange("p a b s -> p (a b s)").rearrange("p (r d) -> p r d", r=ST)
        par_rows = v_att[:, 0, 0:P]
        lam_in = v_gate[:, 0, 0:4 * L * HD].rearrange("p (v l d) -> p v l d", v=4, l=L)
        lam_prod = v_gate[:, 1, 0:2 * L * HD].rearrange("p (v l d) -> p v l d", v=2, l=L)
        o_diag = prob[:, :, :, :].rearrange("p b j s -> p (b j) s").rearrange("p h (r q) -> p h r q", r=ST)

        banks = ctx.enter_context(nc.psum_tensor("banks", [P, 8, 512], F32))
        bank = [banks[:, i, :] for i in range(8)]
        b_tr = [bank[i][:, :].rearrange("p (r q) -> p r q", r=ST) for i in range(8)]
        SQ_BANK, BC_BANK, SSQ_BANK = 5, 4, 7
        X_BANKS = [4, 7]
        T_BANK, WS_BANK, O_BANK = 2, 1, 3
        U_BANKS = [0, 1, 0, 1]
        GATE_BANKS = [0, 0, 1, 0]
        GATE_STEPS = {10: 0, 12: 1, 13: 2, 14: 3}
        OUT_BANKS = [1, 0, 2, 3]
        ssq_col = bank[SSQ_BANK][:, 0:ST]
        ossq_col = bank[O_BANK][:, 0:ST]

        x_landed = [sem(f"x_landed{r}") for r in range(ST)]
        par_landed = sem("par_landed")
        lam_landed = sem("lam_landed")
        consts_ready = sem("consts_ready")
        ident_ready = sem("ident_ready")
        par_turned = sem("par_turned")
        par_ready = sem("par_ready")
        lam_steps = sem("lam_steps")
        lam_ready = sem("lam_ready")
        lam_exp_ready = sem("lam_exp_ready")
        par_loaded = sem("par_loaded")
        x_turned = sem("x_turned")
        w_landed = [sem("w_landed0"), sem("w_landed1")]
        w_hi_ready = sem("w_hi_ready")
        w_ready = sem("w_ready")
        w_done = sem("w_done")
        x_ready = sem("x_ready")
        xg_hi_ready = sem("xg_hi_ready")
        xg_ready = sem("xg_ready")
        sq_ready = sem("sq_ready")
        sq_summed = sem("sq_summed")
        ssq_ready = sem("ssq_ready")
        root_ready = sem("root_ready")
        rcol_ready = sem("rcol_ready")
        diag_ready = sem("diag_ready")
        bc_ready = sem("bc_ready")
        rstd_x_ready = sem("rstd_x_ready")
        tables_landed = sem("tables_landed")
        trig_scaled = sem("trig_scaled")
        qk_swapped = sem("qk_swapped")
        qk_cos = sem("qk_cos")
        qk_sin = sem("qk_sin")
        qk_rotated = sem("qk_rotated")
        vg_gelu = sem("vg_gelu")
        vg_stats = sem("vg_stats")
        vg_var = sem("vg_var")
        ln_root_ready = sem("ln_root_ready")
        ln_rs_ready = sem("ln_rs_ready")
        xhat_ready = sem("xhat_ready")
        va_done = sem("va_done")
        ws_turned = sem("ws_turned")
        ws_copied = sem("ws_copied")
        ws_masked = sem("ws_masked")
        ws_summed = sem("ws_summed")
        add_ready = sem("add_ready")
        u_scaled = sem("u_scaled")
        u_gelu = sem("u_gelu")
        gm_ready = sem("gm_ready")
        gm_added = sem("gm_added")
        ya_mul = sem("ya_mul")
        ya_hi = sem("ya_hi")
        ya_ready = sem("ya_ready")
        sc_ready = sem("sc_ready")
        sc_masked = sem("sc_masked")
        max_ready = sem("max_ready")
        nmax_ready = sem("nmax_ready")
        exp_done = sem("exp_done")
        rinv_ready = sem("rinv_ready")
        w1_ready = sem("w1_ready")
        p1_scaled = sem("p1_scaled")
        a_ready = sem("a_ready")
        at_ready = sem("at_ready")
        at_copied = sem("at_copied")
        pv_ready = sem("pv_ready")
        o_copied = sem("o_copied")
        o_squared = sem("o_squared")
        ossq_ready = sem("ossq_ready")
        o_mean_ready = sem("o_mean_ready")
        o_root_ready = sem("o_root_ready")
        o_rs_ready = sem("o_rs_ready")
        o_diag_ready = sem("o_diag_ready")
        o_bc_ready = sem("o_bc_ready")
        yb_mul = sem("yb_mul")
        yb_hi = sem("yb_hi")
        yb_ready = sem("yb_ready")
        y_copied = sem("y_copied")
        y_scaled = sem("y_scaled")
        g_scaled = sem("g_scaled")
        up_scaled = sem("up_scaled")
        silu_done = sem("silu_done")
        prod_done = sem("prod_done")
        hid_hi_ready = sem("hid_hi_ready")
        hid_ready = sem("hid_ready")
        out_turned = sem("out_turned")
        out_copied = sem("out_copied")
        out_stored = sem("out_stored")

        def cut(l, c, halves=2):
            return at(l, 2 * NC, 2 * c) + 4 + halves

        def high_cut(l, c, halves=2):
            return at(l, 2 * NC, 2 * c) + halves

        def done(l, c, eighths=8):
            return at(l, 8 * NC, 8 * c) + 16 + eighths

        def landed(l, c, pair=0):
            return at(l, 16 * NC, 32 * (c // 2 + 1)) + 32 * pair

        GR_MIX, GR_X1, GR_FFN, GR_X2 = 1, 2, 3, 4

        w_in_v = w_in.rearrange("l (k p) c -> l p k c", p=P)
        w_out_v = w_out.rearrange("l (k p) c -> l p k c", p=P)
        w_gu_v = w_gate_up.rearrange("l (k p) c -> l p k c", p=P)
        w_dn_v = w_down.rearrange("l (k p) c -> l p k c", p=P)

        def wide(b):
            return raw[:, b, :].rearrange("p (k c) -> p k c", c=4 * P)

        def tall(b):
            return raw[:, b, :].rearrange("p (k c) -> p k c", c=2 * P)

        def down(b):
            return raw[:, b, 0:CD].rearrange("p (k c) -> p k c", c=P)

        def raw_half(kind, b, h):
            if kind == "tall":
                return tall(b)[:, :, h * P:(h + 1) * P]
            if kind == "wide":
                return wide(b)[:, 2 * h:2 * h + 2, :]
            return down(b)

        def part(t, kind, b, h=0):
            if kind == "down":
                return t[:, b, :, :].rearrange("p h e -> p (h e)")[:, 0:CD].rearrange("p (k c) -> p k c", c=P)
            return t[:, b, h, :].rearrange("p (k c) -> p k c", c=P if kind == "tall" else 4 * P)

        block = ctx.enter_context(nc.Block())

        @block.sync
        def _(sp):
            for r in range(ST):
                sp.dma_start(rows[:, r, :], x[0, r * P:(r + 1) * P, :]).then_inc(x_landed[r], 16)

            def load(l, c, b, halves):
                sp.wait_ge(w_ready, cut(l, c - 2))
                for dst, src in halves:
                    sp.dma_start(dst, src).then_inc(w_landed[b], 16)

            def load_wide(l, c, col, k0):
                w = wide(c % 2)
                load(l, c, c % 2, [(w[:, k:k + 2, :], w_in_v[l, :, k0 + k:k0 + k + 2, col:col + 4 * P])
                                   for k in (0, 2)])

            def load_tall(l, c, src, col):
                w = tall(c % 2)
                load(l, c, c % 2, [(w[:, k:k + 4, :], src[:, k:k + 4, col:col + 2 * P]) for k in (4, 0)])

            load_tall(0, C_QK, w_in_v[0], K0)
            load_tall(0, C_QK + 1, w_in_v[0], Q0)
            with sp.Fori(0, L) as l:
                load_tall(l, C_QK + 2, w_in_v[l], K0 + 2 * P)
                load_tall(l, C_QK + 3, w_in_v[l], Q0 + 2 * P)
                for n in range(2):
                    load_wide(l, C_VG + n, V0, 4 * n)
                for n in range(2):
                    load_wide(l, C_VA + n, A0, 4 * n)
                for n in range(2):
                    load_tall(l, C_U + n, w_in_v[l], U0 + n * 2 * P)
                for n in range(4):
                    load_tall(l, C_OUT + n, w_out_v[l], n * 2 * P)
                with sp.Fori(0, FT // 2) as i:
                    for b in range(2):
                        w = tall(b)
                        load(l, C_GU + 2 * i + b, b,
                             [(w[:, :, j * P:(j + 1) * P],
                               w_gu_v[l, :, :, bass.ds((2 * i + b) * P + j * FF, P)]) for j in (0, 1)])
                with sp.Fori(0, KT) as t:
                    for b in range(2):
                        w = down(b)
                        load(l, C_DOWN + 2 * t + b, b,
                             [(w[:, k:m, :], w_dn_v[l, :, b * FH + k:b * FH + m, bass.ds(t * P, P)])
                              for k, m in ((0, FH // 2), (FH // 2, FH))])
                load_tall(l, NC, w_in_v[L - 1], K0)
                load_tall(l, NC + 1, w_in_v[L - 1], Q0)
            for r in range(ST):
                sp.wait_ge(out_copied, 2 * (r + 1))
                sp.dma_start(out[0, r * P:(r + 1) * P, :], rows[:, r, :]).then_inc(out_stored, 16)
            sp.wait_ge(out_stored, 16 * ST)
            for b in range(2):
                sp.wait_ge(w_landed[b], 32 * (L * NC // 2 + 1))

        @block.gpsimd
        def _(pool):
            nc.gpsimd.memset(ident[:, :], 0.0).then_inc(w_ready, 4)
            pool.wait_ge(w_ready, 4)
            nc.gpsimd.affine_select(out=ident[:, :], in_=ident[:, :], compare_op=ALU.not_equal, fill=1.0, base=0,
                                    pattern=[[-1, P]], channel_multiplier=1).then_inc(ident_ready, 1)

            def low(l, c, b, h, kind):
                pool.wait_ge(w_hi_ready, high_cut(l, c, 2 if kind == "down" else h + 1))
                nc.gpsimd.tensor_tensor(part(w_lo, kind, b, h), raw_half(kind, b, h),
                                        part(w_hi, kind, b, h).bitcast(F32), ALU.subtract)\
                    .then_inc(w_ready, 2 if kind == "down" else 1)

            def low_halves(l, c, b, kind):
                for h in range(2):
                    low(l, c, b, h, kind)

            for c in range(2):
                low_halves(0, c, c, "tall")
            with pool.Fori(0, L) as l:
                for c in range(C_QK + 2, C_GU):
                    low_halves(l, c, c % 2, "wide" if C_VG <= c < C_U else "tall")
                with pool.Fori(0, FT // 2) as i:
                    for b in range(2):
                        low_halves(l, C_GU + b + 2 * i, b, "tall")
                with pool.Fori(0, KT) as t:
                    for b in range(2):
                        low(l, C_DOWN + b + 2 * t, b, 0, "down")
                for c in range(2):
                    low_halves(l, NC + c, c, "tall")

        @block.tensor
        def _(pe):
            mm, tr = nc.tensor.matmul, nc.tensor.transpose

            def product(o, stat, mov, first, last):
                mm(o, stat[0], mov[0], start=first, stop=False)
                mm(o, stat[1], mov[0], start=False, stop=False)
                return mm(o, stat[0], mov[1], start=False, stop=last)

            def xg_pair(k, s=slice(None)):
                return xg_hi[:, k, s], xg_lo[:, k, s]

            def tall_pair(b, k, j):
                return [part(w, "tall", b, j)[:, k, :] for w in (w_hi, w_lo)]

            def pair_of_chunks(l, c, into, operand_ready, between):
                pe.wait_ge(w_ready, cut(l, c + 1, 1))
                for k in range(KT):
                    operand_ready(k)
                    for n in range(3):
                        last = product(bank[into[n]][:, :], tall_pair((c + n // 2) % 2, k, n % 2), xg_pair(k),
                                       k == 0, k == KT - 1)
                        if k == KT - 1:
                            last.then_inc(w_done, 4)
                between()
                pe.wait_ge(w_ready, cut(l, c + 1, 2))
                tall_tile((c + 1) % 2, 1, into[3]).then_inc(w_done, 4)

            def tall_tile(b, j, o, ks=range(KT)):
                for k in ks:
                    last = product(bank[o][:, :], tall_pair(b, k, j), xg_pair(k), k == 0, k == KT - 1)
                return last

            def sum_columns(l, group):
                pe.wait_ge(sq_summed, at(l, 4 * KT, KT * (group + 1)))
                for r in range(ST):
                    last = mm(ssq_col[:, r:r + 1], sq_sum[:, r * P:(r + 1) * P], ones[:, 0:1], start=True, stop=True)
                last.then_inc(ssq_ready, 1)

            def broadcast(l, group):
                pe.wait_ge(diag_ready, at(l, 4, group + 1))
                mm(bank[BC_BANK][:, :], ones[:, :], diag[:, :, :], start=True, stop=True).then_inc(bc_ready, 1)

            pe.wait_ge(ident_ready, 1)
            pe.wait_ge(par_landed, 16 * PAR_DMAS)
            tr(bank[2][:, 0:PAR_ROWS], par_rows[0:PAR_ROWS, :], ident[0:PAR_ROWS, 0:PAR_ROWS]).then_inc(par_turned, 1)
            for r in range(ST):
                pe.wait_ge(x_landed[r], 16)
            for k in range(KT):
                if k >= 2:
                    pe.wait_ge(x_ready, k - 1)
                for r in range(ST):
                    last = tr(b_tr[X_BANKS[k % 2]][:, r, :], rows[:, r, k * P:(k + 1) * P], ident[:, :])
                last.then_inc(x_turned, 1)

            with pe.Fori(0, L) as l:
                pair_of_chunks(l, C_QK, QK_BANKS[0:4],
                               lambda k: pe.wait_ge(xg_ready, at(l, 2 * KT, k + 1)),
                               lambda: sum_columns(l, 0))
                broadcast(l, 0)
                for j in range(2):
                    pe.wait_ge(w_ready, cut(l, C_QK + 2, j + 1))
                    tall_tile(0, j, QK_BANKS[4 + j]).then_inc(w_done, 4)
                for j in range(2):
                    pe.wait_ge(w_ready, cut(l, C_QK + 3, j + 1))
                    pe.wait_ge(qk_cos, at(l, 2 * H, j + 1))
                    tall_tile(1, j, QK_BANKS[6 + j]).then_inc(w_done, 4)

                def values(c, into, bank_free):
                    for n in range(4):
                        b, h = n // 2, n % 2
                        pe.wait_ge(w_ready, cut(l, c + b, h + 1))
                        for r in range(ST):
                            if n == 0:
                                bank_free(r)
                            for k in range(2):
                                w = [part(t, "wide", b, h)[:, k, :] for t in (w_hi, w_lo)]
                                last = product(bank[into[r]][:, :],
                                               xg_pair(2 * n + k, slice(r * P, (r + 1) * P)), w,
                                               n == 0 and k == 0, n == 3 and k == 1)
                            if n == 3:
                                last.then_inc(w_done, 1)
                        if n < 3:
                            last.then_inc(w_done, 4)

                def gate_bank_free(r):
                    if r == 0:
                        pe.wait_ge(rstd_x_ready, at(l, 2, 1))
                    elif r < 3:
                        pe.wait_ge(qk_cos, at(l, 2 * H, 4 + r))

                values(C_VG, [4, 5, 6, 7], gate_bank_free)
                values(C_VA, [0, 1, 2, 3], lambda r: pe.wait_ge(qk_cos, at(l, 2 * H, 2 * H)))

                def scores(n):
                    h, i = divmod(n, ST)
                    w = (i + 1) * P
                    if i == 0:
                        pe.wait_ge(qk_rotated, at(l, 2 * H, 4 if h < 2 else 8))
                    if n < 2:
                        pe.wait_ge(vg_gelu, at(l, ST, 2 * n + 2))
                    else:
                        pe.wait_ge(exp_done, at(l, 2 * NS, 2 * (n - 1)))
                    for j in range(2):
                        ps = slice(j * HD, (j + 1) * HD)
                        last = mm(bank[4 + 2 * (n % 2) + j][:, 0:w], q_rot[ps, h, i * P:(i + 1) * P],
                                  k_rot[ps, h, 0:w], start=True, stop=True)
                    last.then_inc(sc_ready, 1)

                def turn(n):
                    i = n % ST
                    pe.wait_ge(a_ready, at(l, NS, n + 1))
                    if n == 0:
                        pe.wait_ge(va_done, at(l, ST, ST))
                    else:
                        pe.wait_ge(at_copied, at(l, NS, n))
                    for k in range(i + 1):
                        last = tr(b_tr[T_BANK][:, k, :], attn[:, n % 2, k * P:(k + 1) * P], ident[:, :])
                    last.then_inc(at_ready, 1)

                def weigh(h):
                    pe.wait_ge(at_copied, at(l, NS, ST * (h + 1)))
                    if h:
                        pe.wait_ge(o_mean_ready, at(l, H, h))
                    for k in range(ST):
                        last = mm(bank[O_BANK][:, k * P:S], v_att[:, k, h * P:(h + 1) * P],
                                  attnT[:, h % 2, k, k * P:S], start=(k == 0), stop=(k == ST - 1))
                    last.then_inc(pv_ready, 1)

                def head_squares(h):
                    pe.wait_ge(o_squared, at(l, H, h + 1))
                    for r in range(ST):
                        last = mm(ossq_col[:, r:r + 1], o_sq[:, r * P:(r + 1) * P], ones[:, 0:1],
                                  start=True, stop=True)
                    last.then_inc(ossq_ready, 1)

                def head_broadcast(h):
                    pe.wait_ge(o_diag_ready, at(l, H, h + 1))
                    mm(bank[4 + h][:, :], ones[:, :], o_diag[:, h, :, :], start=True, stop=True)\
                        .then_inc(o_bc_ready, 1)

                def u_third(n):
                    t, third = divmod(n, 3)
                    if third == 0:
                        pe.wait_ge(w_ready, cut(l, C_U + t // 2, t % 2 + 1))
                        if t == 0:
                            pe.wait_ge(va_done, at(l, ST, 1))
                        elif t == 1:
                            pe.wait_ge(add_ready, l + 1)
                        else:
                            pe.wait_ge(u_scaled, at(l, G, t - 1))
                    ks = [range(0, 3), range(3, 6), range(6, KT)][third]
                    last = tall_tile(t // 2 % 2, t % 2, U_BANKS[t], ks)
                    if third == 2:
                        last.then_inc(w_done, 4)

                def gate(g):
                    if g == 0:
                        pe.wait_ge(xhat_ready, at(l, ST, ST))
                    if g == 0 or g == 2:
                        pe.wait_ge(u_scaled, at(l, G, 3 if g == 0 else 4))
                    else:
                        pe.wait_ge(gm_added, at(l, G, 1 if g == 1 else 2))
                    for n in range(ST):
                        last = mm(b_tr[GATE_BANKS[g]][:, n, :], v_gate[:, n, g * P:(g + 1) * P], wsT[:, g, :],
                                  start=True, stop=True)
                    last.then_inc(gm_ready, 1)

                def out_part(n, ks):
                    if ks[0] == 0:
                        pe.wait_ge(w_ready, cut(l, C_OUT + n // 2, n % 2 + 1))
                        if n < 2:
                            pe.wait_ge(gm_added, at(l, G, 3 + n))
                        else:
                            pe.wait_ge(at_copied, at(l, NS, NS))
                    for k in ks:
                        pe.wait_ge(ya_ready, at(l, G, k + 1))
                        product(bank[OUT_BANKS[n]][:, :], tall_pair(n // 2, k, n % 2), xg_pair(k), k == 0, False)

                for n in range(NS + 5):
                    if n < NS:
                        scores(n)
                    if n < 3 * G:
                        u_third(n)
                    if n in GATE_STEPS:
                        gate(GATE_STEPS[n])
                    if NS <= n < NS + 4:
                        out_part((n - NS) // 2, range(2 * (n % 2), 2 * (n % 2) + 2))
                    if n == 0:
                        pe.wait_ge(tables_landed, at(l, 16 * TABLES, 16 * TABLES))
                        pe.wait_ge(va_done, at(l, ST, ST))
                        for g in range(G):
                            last = tr(b_tr[WS_BANK][:, g, :], ws[:, g, :], ident[:, :])
                        last.then_inc(ws_turned, 1)
                    if n == 1:
                        pe.wait_ge(ws_masked, l + 1)
                        mm(bank[WS_BANK][:, :], ones[:, :], wsT[:, :, :], start=True, stop=True)\
                            .then_inc(ws_summed, 1)
                    if 2 <= n < NS + 2:
                        turn(n - 2)
                    if n >= 6 and n % ST == 2:
                        weigh((n - 6) // ST)
                    if n >= 8 and n % ST == 0 and n <= NS:
                        head_squares((n - 8) // ST)
                    if n == NS + 3:
                        head_squares(H - 1)
                        for h in range(H - 1):
                            head_broadcast(h)
                        out_part(2, range(G))
                        head_broadcast(H - 1)

                for k in range(G, KT):
                    pe.wait_ge(yb_ready, at(l, H, k - G + 1))
                    for n in range(3):
                        last = product(bank[OUT_BANKS[n]][:, :], tall_pair(n // 2, k, n % 2), xg_pair(k),
                                       False, k == KT - 1)
                        if k == KT - 1:
                            last.then_inc(w_done, 4)
                pe.wait_ge(w_ready, cut(l, C_OUT + 1, 2))
                pe.wait_ge(o_mean_ready, at(l, H, H))
                tall_tile(1, 1, OUT_BANKS[3]).then_inc(w_done, 4)
                for n in range(4, KT):
                    pe.wait_ge(w_ready, cut(l, C_OUT + n // 2, n % 2 + 1))
                    pe.wait_ge(y_copied, at(l, 2 * KT, n - 3))
                    tall_tile(n // 2 % 2, n % 2, OUT_BANKS[n - 4]).then_inc(w_done, 4)
                sum_columns(l, GR_MIX)
                broadcast(l, GR_MIX)

                def hidden_tile(c, b, into):
                    for j in range(2):
                        pe.wait_ge(w_ready, cut(l, c, j + 1))
                        tall_tile(b, j, into[j]).then_inc(w_done, 4)

                pair_of_chunks(l, C_GU, [0, 1, 2, 3],
                               lambda k: pe.wait_ge(xg_ready, at(l, 2 * KT, KT + k + 1)),
                               lambda: sum_columns(l, GR_X1))
                broadcast(l, GR_X1)
                hidden_tile(C_GU + 2, 0, [5, 6])
                pe.wait_ge(up_scaled, at(l, FT, 1))
                hidden_tile(C_GU + 3, 1, [0, 1])
                with pe.Fori(0, (FT - 4) // 2) as i:
                    pe.wait_ge(up_scaled, at(l, FT, 3) + 2 * i)
                    hidden_tile(C_GU + 4 + 2 * i, 0, [2, 3])
                    pe.wait_ge(up_scaled, at(l, FT, 4) + 2 * i)
                    hidden_tile(C_GU + 5 + 2 * i, 1, [0, 1])

                def half_tile(c, b, o):
                    pe.wait_ge(w_ready, cut(l, c))
                    w = [part(t, "down", b) for t in (w_hi, w_lo)]
                    for k in range(FH):
                        f = b * FH + k
                        last = product(bank[o][:, :], [v[:, k, :] for v in w], (hid_hi[:, f, :], hid_lo[:, f, :]),
                                       f == 0, f == FT - 1)
                    last.then_inc(w_done, 8)

                with pe.Fori(0, KT // 2) as i:
                    for j in range(2):
                        pe.wait_ge(y_copied, at(l, 2 * KT, KT - 1 + j) + 2 * i)
                        for b in range(2):
                            if j == 0 and b == 0:
                                pe.wait_ge(up_scaled, at(l, FT, FT - 1))
                                pe.wait_ge(hid_ready, at(l, FT, FH))
                            if j == 0 and b == 1:
                                pe.wait_ge(hid_ready, at(l, FT, FT))
                            half_tile(C_DOWN + 4 * i + 2 * j + b, b, 2 + j)
                sum_columns(l, GR_FFN)
                broadcast(l, GR_FFN)

            for r in range(ST):
                for half in range(2):
                    n = 2 * r + half
                    if n >= 2:
                        pe.wait_ge(out_copied, n - 1)
                    for k in range(4):
                        if r == 0:
                            pe.wait_ge(x_ready, 2 * L * KT + 4 * half + k + 1)
                        last = tr(b_tr[n % 2][:, k, :], xT[:, 4 * half + k, r * P:(r + 1) * P], ident[:, :])
                    last.then_inc(out_turned, 1)

        def ffn_banks(f):
            return (5, 6) if f == 2 else (2, 3) if f == 1 or (f > 2 and f % 2 == 0) else (0, 1)

        @block.scalar
        def _(act):
            fn = nc.scalar.activation

            n_par = 0
            for l in range(L):
                base = l * NEG_LAM
                nxt = min(l + 1, L - 1)
                for at_row, src, n in ((POST_MIX, post_mix_g[l], KT), (PRE_FFN, pre_ffn_g[l], KT),
                                       (POST_FFN, post_ffn_g[l], KT), (NEXT_MIX, pre_mix_g[nxt], KT),
                                       (LN_G, gmlp_ln_g[l], G), (LN_B, gmlp_ln_b[l], G), (SUBLN, subln_g[l], 1)):
                    act.dma_start(par_rows[base + at_row:base + at_row + n, :],
                                  src.rearrange("(k p) -> k p", k=n)).then_inc(par_landed, 16)
                    n_par += 1
            act.dma_start(par_rows[L * NEG_LAM:PAR_ROWS, :],
                          pre_mix_g[0].rearrange("(k p) -> k p", k=KT)).then_inc(par_landed, 16)
            assert n_par + 1 == PAR_DMAS
            for n, v in enumerate((lambda_q1, lambda_q2, lambda_k1, lambda_k2)):
                act.dma_start(lam_in[:, n, :, :], v.partition_broadcast(P)).then_inc(lam_landed, 16)

            def high(l, c, h, b, kind, pair=0):
                act.wait_ge(w_landed[b], landed(l, c, pair))
                act.wait_ge(w_done, done(l, c - 2, 8 if kind == "down" else 4 * h + 4) + 16 * pair)
                fn(part(w_hi, kind, b, h), raw_half(kind, b, h), ACT.Copy)\
                    .then_inc(w_hi_ready, 2 if kind == "down" else 1)

            def gain_and_square(l, tiles_before, group, k, gain):
                act.wait_ge(x_ready, at(l, 2 * KT, tiles_before + k + 1))
                fn(xg_hi[:, k, :], xT[:, k, :], ACT.Copy, scale=gain).then_inc(xg_hi_ready, 1)
                square(l, group, k, xT[:, k, :])

            def square(l, group, k, src):
                if group or k >= 2:
                    act.wait_ge(sq_summed, at(l, 4 * KT, KT * group + k - 1))
                fn(bank[SQ_BANK + k % 2][:, :], src, ACT.Square).then_inc(sq_ready, 1)

            def root_of_mean(l, group):
                act.wait_ge(ssq_ready, at(l, 4, group + 1))
                fn(root[:, :], ssq_col, ACT.Sqrt, scale=1.0 / D, bias=eps[:, :]).then_inc(root_ready, 1)

            def copy_rstd_x(l, group):
                act.wait_ge(bc_ready, at(l, 4, group + 1))
                fn(rstd_x[:, :], bank[BC_BANK][:, :], ACT.Copy).then_inc(rstd_x_ready, 1)

            act.wait_ge(w_ready, 4)
            for c in range(2):
                for h in range(2):
                    high(0, c, h, c, "tall")
            act.wait_ge(lam_ready, 1)
            fn(lam_exp[:, :, :], lam_sum[:, :, :], ACT.Exp).then_inc(lam_exp_ready, 1)
            act.wait_ge(par_ready, PAR_STEPS)
            act.wait_ge(consts_ready, 2)
            for k in range(KT):
                gain_and_square(0, 0, 0, k, gain0[:, k:k + 1])

            with act.Fori(0, L) as l:
                act.wait_ge(w_done, done(l, -1))
                act.dma_start(trig[:, :, :], rope.rearrange("t p s -> p t s")).then_inc(tables_landed, 16)
                act.dma_start(ws[:, :, :], gmlp_ws[l].rearrange("g t s -> t g s")).then_inc(tables_landed, 16)
                act.dma_start(g_bias[:, :, :], gmlp_b[l].partition_broadcast(P)).then_inc(tables_landed, 16)

                root_of_mean(l, 0)
                high(l, C_QK + 2, 0, 0, "tall")
                high(l, C_QK + 2, 1, 0, "tall")
                high(l, C_QK + 3, 0, 1, "tall")
                copy_rstd_x(l, 0)
                high(l, C_QK + 3, 1, 1, "tall")
                for n in range(2 * H):
                    act.wait_ge(w_done, done(l, C_QK + n // 2, 4 * (n % 2) + 4))
                    if n >= 2:
                        act.wait_ge(qk_rotated, at(l, 2 * H, n - 1))
                    q = P // 4
                    for a in range(4):
                        src = a + 1 if a % 2 == 0 else a - 1
                        last = fn(swap[a * q:(a + 1) * q, n % 2, :],
                                  bank[QK_BANKS[n]][src * q:(src + 1) * q, :], ACT.Copy)
                    last.then_inc(qk_swapped, 1)
                    if n >= 4:
                        high(l, C_QK + 2 + n // 2, n % 2, n // 2 % 2, "wide")
                high(l, C_VG + 2, 0, 0, "wide")
                high(l, C_VG + 2, 1, 0, "wide")
                high(l, C_VG + 3, 0, 1, "wide")
                for r in range(ST):
                    act.wait_ge(w_done, done(l, C_VG + 1, 4 + r + 1))
                    fn(v_gate[:, r, :], bank[4 + r][:, :], ACT.Gelu, scale=rcol[:, 0, r:r + 1]).then_inc(vg_gelu, 1)
                high(l, C_VG + 3, 1, 1, "wide")
                high(l, C_VA + 2, 0, 0, "tall")
                high(l, C_VA + 2, 1, 0, "tall")
                high(l, C_VA + 3, 0, 1, "tall")
                for r in range(ST):
                    act.wait_ge(w_done, done(l, C_VA + 1, 4 + r + 1))
                    fn(v_att[:, r, :], bank[r][:, :], ACT.Copy, scale=rcol[:, 0, r:r + 1]).then_inc(va_done, 1)
                high(l, C_VA + 3, 1, 1, "tall")
                act.wait_ge(vg_var, at(l, ST, ST))
                fn(ln_root[:, :], mv[:, :, 1], ACT.Sqrt, bias=eps[:, :]).then_inc(ln_root_ready, 1)

                def exponentials(n):
                    w = (n % ST + 1) * P
                    act.wait_ge(nmax_ready, at(l, NS, n + 1))
                    if n >= 2:
                        act.wait_ge(a_ready, at(l, NS, n - 1))
                    for j in range(2):
                        fn(prob[:, n % 2, j, 0:w], bank[4 + 2 * (n % 2) + j][:, 0:w], ACT.Exp, scale=SCALE,
                           bias=nmx[:, n % 2, j:j + 1], accum_out=psumr[:, n % 2, j:j + 1]).then_inc(exp_done, 1)

                def copy_turned(n):
                    h, i = divmod(n, ST)
                    act.wait_ge(at_ready, at(l, NS, n + 1))
                    if h >= 2 and i == 0:
                        act.wait_ge(pv_ready, at(l, H, h - 1))
                    fn(attnT[:, h % 2, 0:i + 1, i * P:(i + 1) * P], b_tr[T_BANK][:, 0:i + 1, :], ACT.Copy)\
                        .then_inc(at_copied, 1)

                def copy_head(h):
                    act.wait_ge(pv_ready, at(l, H, h + 1))
                    fn(oT[:, h, :], bank[O_BANK][:, :], ACT.Copy).then_inc(o_copied, 1)
                    if h:
                        act.wait_ge(ossq_ready, at(l, H, h))
                    fn(o_sq[:, :], bank[O_BANK][:, :], ACT.Square).then_inc(o_squared, 1)

                def mean_of_head(h):
                    act.wait_ge(ossq_ready, at(l, H, h + 1))
                    fn(o_mean[:, h, :], ossq_col, ACT.Copy, scale=1.0 / P).then_inc(o_mean_ready, 1)

                def head_roots(n, lo, hi):
                    act.wait_ge(o_mean_ready, at(l, H, hi))
                    fn(o_root[:, lo:hi, :], o_mean[:, lo:hi, :], ACT.Sqrt, bias=eps[:, :]).then_inc(o_root_ready, 1)

                def gated_high(g):
                    act.wait_ge(ya_mul, at(l, G, g + 1))
                    fn(xg_hi[:, g, :], uT[:, g, :], ACT.Copy).then_inc(ya_hi, 1)

                def head_high(h):
                    act.wait_ge(yb_mul, at(l, H, h + 1))
                    fn(xg_hi[:, G + h, :], oT[:, h, :], ACT.Copy).then_inc(yb_hi, 1)

                for n in range(NS + 2):
                    if n < NS:
                        exponentials(n)
                    if n and n % 3 == 0 and n <= 3 * G:
                        t = n // 3 - 1
                        high(l, C_U + 2 + t // 2, t % 2, t // 2, "tall")
                    if n == 0:
                        act.wait_ge(ws_turned, l + 1)
                        fn(wsT[:, :, :], b_tr[WS_BANK][:, :, :], ACT.Copy).then_inc(ws_copied, 1)
                    if n >= 2:
                        copy_turned(n - 2)
                    if n == 3 * G:
                        for g in range(G):
                            act.wait_ge(u_scaled, at(l, G, g + 1))
                            fn(uT[:, g, :], uT[:, g, :], ACT.Gelu).then_inc(u_gelu, 1)
                    if 3 * G < n <= NS:
                        gated_high(n - 3 * G - 1)
                    if n >= 6 and n % ST == 2:
                        copy_head((n - 6) // ST)
                    if n >= 8 and n % ST == 0:
                        mean_of_head((n - 8) // ST)
                head_roots(0, 0, H - 1)
                copy_head(H - 1)
                mean_of_head(H - 1)
                head_roots(1, H - 1, H)
                for h in range(H):
                    head_high(h)

                def output_tile(t, group, o):
                    square(l, group, t, bank[o][:, :])
                    fn(yT[:, t, :], bank[o][:, :], ACT.Copy).then_inc(y_copied, 1)

                for t in range(KT):
                    high(l, C_OUT + 2 + t // 2, t % 2, t // 2 % 2, "tall")
                    output_tile(t, GR_MIX, OUT_BANKS[t % 4])
                root_of_mean(l, GR_MIX)
                for k in range(KT):
                    gain_and_square(l, KT, GR_X1, k, par[:, PRE_FFN + k:PRE_FFN + k + 1])
                root_of_mean(l, GR_X1)
                high(l, C_GU + 2, 0, 0, "tall")
                high(l, C_GU + 2, 1, 0, "tall")
                high(l, C_GU + 3, 0, 1, "tall")
                copy_rstd_x(l, GR_X1)
                high(l, C_GU + 3, 1, 1, "tall")

                def hidden(f, b):
                    act.wait_ge(g_scaled, at(l, FT, 1) + f)
                    fn(gate_t[:, b, :], gate_t[:, b, :], ACT.Silu).then_inc(silu_done, 1)
                    act.wait_ge(prod_done, at(l, FT, 1) + f)
                    fn(hid_hi[:, f, :], up_t[:, b, :], ACT.Copy).then_inc(hid_hi_ready, 1)

                hidden(0, 0)
                hidden(1, 1)
                with act.Fori(0, (FT - 4) // 2) as i:
                    for b in range(2):
                        high(l, C_GU + 4 + b, 0, b, "tall", i)
                        high(l, C_GU + 4 + b, 1, b, "tall", i)
                        hidden(2 * i + 2 + b, b)
                for b in range(2):
                    high(l, C_DOWN + b, 0, b, "down")
                    hidden(FT - 2 + b, b)
                for c in range(2 * KT):
                    if c < 2 * KT - 2:
                        high(l, C_DOWN + 2 + c, 0, c % 2, "down")
                    else:
                        for h in range(2):
                            high(l, C_DOWN + 2 + c, h, c % 2, "tall")
                    if c % 2:
                        output_tile(c // 2, GR_FFN, 2 + c // 2 % 2)
                root_of_mean(l, GR_FFN)
                for k in range(KT):
                    gain_and_square(l, 2 * KT, GR_X2, k, par[:, NEXT_MIX + k:NEXT_MIX + k + 1])

        @block.vector
        def _(dve):
            tt, ts, stt, copy = (nc.vector.tensor_tensor, nc.vector.tensor_scalar, nc.vector.scalar_tensor_tensor,
                                 nc.vector.tensor_copy)
            nc.vector.memset(ones[:, :], 1.0).then_inc(w_done, 16)
            nc.vector.memset(eps[:, :], EPS).then_inc(consts_ready, 2)

            dve.wait_ge(lam_landed, 16 * 4)
            tt(lam_prod, lam_in[:, 0:2, :, :], lam_in[:, 2:4, :, :], ALU.mult).then_inc(lam_steps, 1)
            dve.wait_ge(lam_steps, 1)
            nc.vector.tensor_reduce(lam_sum[:, :, :], lam_prod, AX_X, ALU.add).then_inc(lam_ready, 1)
            dve.wait_ge(par_turned, 1)
            copy(par_all[:, :, 0:NEG_LAM], bank[2][:, 0:L * NEG_LAM].rearrange("p (l n) -> p l n", l=L))\
                .then_inc(par_ready, 1)
            copy(gain0[:, :], bank[2][:, L * NEG_LAM:PAR_ROWS]).then_inc(par_ready, 1)
            dve.wait_ge(lam_exp_ready, 1)
            tt(lam_d[:, :], lam_exp[:, 1, :], lam_exp[:, 0, :], ALU.subtract).then_inc(lam_steps, 1)
            dve.wait_ge(lam_steps, 2)
            dve.wait_ge(par_ready, 2)
            for l in range(L):
                ts(par_all[:, l, NEG_LAM:NEG_LAM + 1], lam_d[:, l:l + 1], -LAM_INIT[l], None, ALU.add)\
                    .then_inc(par_ready, 1)
                ts(par_all[:, l, SUBLN:SUBLN + 1], par_all[:, l, SUBLN:SUBLN + 1], 1.0 - LAM_INIT[l], None, ALU.mult)\
                    .then_inc(par_ready, 1)

            def low_part(l, tiles_before, k, gain):
                dve.wait_ge(xg_hi_ready, at(l, 2 * KT, tiles_before + k + 1))
                stt(xg_lo[:, k, :], xT[:, k, :], gain, xg_hi[:, k, :].bitcast(F32), ALU.mult, ALU.subtract)\
                    .then_inc(xg_ready, 1)

            def add_square(l, group, k):
                dve.wait_ge(sq_ready, at(l, 4 * KT, KT * group + k + 1))
                if k == 0:
                    if group:
                        dve.wait_ge(ssq_ready, at(l, 4, group))
                    copy(sq_sum[:, :], bank[SQ_BANK][:, :]).then_inc(sq_summed, 1)
                else:
                    dve.wait_ge(sq_summed, at(l, 4 * KT, KT * group + k))
                    tt(sq_sum[:, :], bank[SQ_BANK + k % 2][:, :], sq_sum[:, :], ALU.add).then_inc(sq_summed, 1)

            def rstd(l, group):
                c = rcol[:, group % 2, :]
                dve.wait_ge(root_ready, at(l, 4, group + 1))
                nc.vector.reciprocal(c, root[:, :]).then_inc(rcol_ready, 1)
                dve.wait_ge(rcol_ready, at(l, 4, group + 1))
                tt(diag[:, :, :], ident[:, :].unsqueeze(1).to_broadcast([P, ST, P]),
                   c.unsqueeze(2).to_broadcast([P, ST, P]), ALU.mult).then_inc(diag_ready, 1)

            def residual(l, tiles_before, k, gain):
                stt(yT[:, k, :], yT[:, k, :], gain, bank[BC_BANK][:, :], ALU.mult, ALU.mult).then_inc(y_scaled, 1)
                dve.wait_ge(y_scaled, at(l, 2 * KT, tiles_before + k + 1))
                tt(xT[:, k, :], xT[:, k, :], yT[:, k, :], ALU.add).then_inc(x_ready, 1)

            def residual_and_low(l, tiles_before, group, gain_y, gain_x):
                dve.wait_ge(bc_ready, at(l, 4, group + 1))
                dve.wait_ge(y_copied, at(l, 2 * KT, tiles_before + KT))
                for k in range(KT + 1):
                    if k < KT:
                        residual(l, tiles_before, k, par[:, gain_y + k:gain_y + k + 1])
                    if k:
                        low_part(l, tiles_before + KT, k - 1, par[:, gain_x + k - 1:gain_x + k])
                        add_square(l, group + 1, k - 1)

            dve.wait_ge(ident_ready, 1)
            for k in range(KT + 1):
                if k < KT:
                    dve.wait_ge(x_turned, k + 1)
                    copy(xT[:, k, :], bank[X_BANKS[k % 2]][:, :]).then_inc(x_ready, 1)
                if k:
                    low_part(0, 0, k - 1, gain0[:, k - 1:k])
                    add_square(0, 0, k - 1)
            dve.wait_ge(par_ready, PAR_STEPS)

            with dve.Fori(0, L) as l:
                dve.wait_ge(xg_ready, at(l, 2 * KT, KT))
                copy(par[:, :], par_all[:, l, :]).then_inc(par_loaded, 1)
                dve.wait_ge(par_loaded, l + 1)
                rstd(l, 0)
                dve.wait_ge(tables_landed, at(l, 16 * TABLES, 16 * TABLES))
                dve.wait_ge(rstd_x_ready, at(l, 2, 1))
                tt(trig[:, :, :], trig[:, :, :], rstd_x[:, :].unsqueeze(1).to_broadcast([P, 2, S]), ALU.mult)\
                    .then_inc(trig_scaled, 1)
                dve.wait_ge(trig_scaled, l + 1)
                for n, (col, h) in enumerate(QK_TILES):
                    dst = (k_rot if col == K0 else q_rot)[:, h, :]
                    dve.wait_ge(qk_swapped, at(l, 2 * H, n + 1))
                    tt(dst, bank[QK_BANKS[n]][:, :], trig[:, 0, :], ALU.mult).then_inc(qk_cos, 1)
                    tt(swap[:, n % 2, :], swap[:, n % 2, :], trig[:, 1, :], ALU.mult).then_inc(qk_sin, 1)
                    dve.wait_ge(qk_cos, at(l, 2 * H, n + 1))
                    dve.wait_ge(qk_sin, at(l, 2 * H, n + 1))
                    tt(dst, dst, swap[:, n % 2, :], ALU.add).then_inc(qk_rotated, 1)
                for r in range(ST):
                    dve.wait_ge(vg_gelu, at(l, ST, r + 1))
                    nc.vector.bn_stats(stats[:, r, :], v_gate[:, r, :]).then_inc(vg_stats, 1)
                dve.wait_ge(vg_stats, at(l, ST, ST))

                def maxima(n):
                    b, w, i = 4 + 2 * (n % 2), (n % ST + 1) * P, n % ST
                    dve.wait_ge(sc_ready, at(l, NS, n + 1))
                    nc.vector.memset(banks[0:CH, b:b + 2, w - CH:w], NEG_INF).then_inc(sc_masked, 1)
                    dve.wait_ge(sc_masked, at(l, NS, n + 1))
                    nc.vector.tensor_reduce(mx[:, :], banks[:, b:b + 2, 0:w], AX_X, ALU.max).then_inc(max_ready, 1)
                    dve.wait_ge(max_ready, at(l, NS, n + 1))
                    ts(nmx[:, n % 2, :], mx[:, :], -SCALE, None, ALU.mult).then_inc(nmax_ready, 1)

                def combine(n):
                    b, w = n % 2, (n % ST + 1) * P
                    dve.wait_ge(exp_done, at(l, 2 * NS, 2 * n + 2))
                    nc.vector.reciprocal(rinv[:, :], psumr[:, b, :]).then_inc(rinv_ready, 1)
                    dve.wait_ge(rinv_ready, at(l, NS, n + 1))
                    tt(w1[:, :], rinv[:, 1:2], par[:, NEG_LAM:NEG_LAM + 1], ALU.mult).then_inc(w1_ready, 1)
                    dve.wait_ge(w1_ready, at(l, NS, n + 1))
                    ts(prob[:, b, 1, 0:w], prob[:, b, 1, 0:w], w1[:, :], None, ALU.mult).then_inc(p1_scaled, 1)
                    dve.wait_ge(p1_scaled, at(l, NS, n + 1))
                    if n >= 2:
                        dve.wait_ge(at_ready, at(l, NS, n - 1))
                    stt(attn[:, b, 0:w], prob[:, b, 0, 0:w], rinv[:, 0:1], prob[:, b, 1, 0:w], ALU.mult, ALU.add)\
                        .then_inc(a_ready, 1)

                def normalize_gate():
                    dve.wait_ge(ln_root_ready, l + 1)
                    nc.vector.reciprocal(ln_rs[:, :], ln_root[:, :]).then_inc(ln_rs_ready, 1)
                    dve.wait_ge(ln_rs_ready, l + 1)
                    for r in range(ST):
                        ts(v_gate[:, r, :], v_gate[:, r, :], mv[:, r, 0:1], ln_rs[:, r:r + 1], ALU.subtract, ALU.mult)\
                            .then_inc(xhat_ready, 1)

                def additive_terms():
                    dve.wait_ge(ws_summed, l + 1)
                    for g in range(G):
                        last = stt(add_t[:, g, :], b_tr[WS_BANK][:, g, :], par[:, LN_B + g:LN_B + g + 1],
                                   g_bias[:, g, :], ALU.mult, ALU.add)
                    last.then_inc(add_ready, 1)

                def scale_u(t):
                    dve.wait_ge(w_done, done(l, C_U + t // 2, 4 * (t % 2) + 4))
                    tt(uT[:, t, :], bank[U_BANKS[t]][:, :], rstd_x[:, :], ALU.mult).then_inc(u_scaled, 1)

                def add_terms(g):
                    dve.wait_ge(gm_ready, at(l, G, g + 1))
                    dve.wait_ge(add_ready, l + 1)
                    stt(v_gate[:, :, g * P:(g + 1) * P], b_tr[GATE_BANKS[g]][:, :, :], par[:, LN_G + g:LN_G + g + 1],
                        add_t[:, g, :].unsqueeze(1).to_broadcast([P, ST, P]), ALU.mult, ALU.add).then_inc(gm_added, 1)

                def gated(g):
                    dve.wait_ge(gm_added, at(l, G, g + 1))
                    dve.wait_ge(u_gelu, at(l, G, g + 1))
                    u = uT[:, g, :].rearrange("p (n t) -> p n t", n=ST)
                    tt(u, u, v_gate[:, :, g * P:(g + 1) * P], ALU.mult).then_inc(ya_mul, 1)

                def gated_low(g):
                    dve.wait_ge(ya_hi, at(l, G, g + 1))
                    tt(xg_lo[:, g, :], uT[:, g, :], xg_hi[:, g, :].bitcast(F32), ALU.subtract).then_inc(ya_ready, 1)

                def head_rs(n, lo, hi):
                    dve.wait_ge(o_root_ready, at(l, 2, n + 1))
                    nc.vector.reciprocal(o_rs[:, lo:hi, :], o_root[:, lo:hi, :]).then_inc(o_rs_ready, 1)
                    dve.wait_ge(o_rs_ready, at(l, 2, n + 1))

                def head_diag(h):
                    tt(o_diag[:, h, :, :], ident[:, :].unsqueeze(1).to_broadcast([P, ST, P]),
                       o_rs[:, h, :].unsqueeze(2).to_broadcast([P, ST, P]), ALU.mult).then_inc(o_diag_ready, 1)

                def head_scale(h):
                    dve.wait_ge(o_copied, at(l, H, h + 1))
                    dve.wait_ge(o_bc_ready, at(l, H, h + 1))
                    stt(oT[:, h, :], oT[:, h, :], par[:, SUBLN:SUBLN + 1], bank[4 + h][:, :], ALU.mult, ALU.mult)\
                        .then_inc(yb_mul, 1)

                def head_low(h):
                    dve.wait_ge(yb_hi, at(l, H, h + 1))
                    tt(xg_lo[:, G + h, :], oT[:, h, :], xg_hi[:, G + h, :].bitcast(F32), ALU.subtract)\
                        .then_inc(yb_ready, 1)

                for n in range(NS + 1):
                    if n and n % 3 == 0 and n <= 3 * G:
                        scale_u(n // 3 - 1)
                    if n - 1 in GATE_STEPS:
                        add_terms(GATE_STEPS[n - 1])
                    if n == 1:
                        dve.wait_ge(ws_copied, l + 1)
                        nc.vector.memset(wsT[CH:P, :, 0:CH], 0.0).then_inc(ws_masked, 1)
                    if n:
                        combine(n - 1)
                    if n < NS:
                        maxima(n)
                    if n == 0:
                        for r in range(ST):
                            nc.vector.bn_aggr(mv[:, r, :], stats[:, r, :]).then_inc(vg_var, 1)
                    if n == 1:
                        normalize_gate()
                    if n == 2:
                        additive_terms()
                    if n > 3 * G:
                        gated(n - 3 * G - 1)
                    if n > 3 * G + 1:
                        gated_low(n - 3 * G - 2)
                gated_low(G - 1)
                head_rs(0, 0, H - 1)
                head_diag(0)
                head_diag(1)
                head_diag(2)
                head_rs(1, H - 1, H)
                head_diag(3)
                head_scale(0)
                head_scale(1)
                head_low(0)
                head_scale(2)
                head_low(1)
                head_scale(3)
                head_low(2)
                head_low(3)

                for t in range(KT):
                    add_square(l, GR_MIX, t)
                rstd(l, GR_MIX)
                residual_and_low(l, 0, GR_MIX, POST_MIX, PRE_FFN)
                rstd(l, GR_X1)
                dve.wait_ge(rstd_x_ready, at(l, 2, 2))

                def hidden(f, b, into):
                    dve.wait_ge(w_done, done(l, C_GU) + 8 * f)
                    tt(gate_t[:, b, :], bank[into[0]][:, :], rstd_x[:, :], ALU.mult).then_inc(g_scaled, 1)
                    tt(up_t[:, b, :], bank[into[1]][:, :], rstd_x[:, :], ALU.mult).then_inc(up_scaled, 1)
                    dve.wait_ge(silu_done, at(l, FT, 1) + f)
                    dve.wait_ge(up_scaled, at(l, FT, 1) + f)
                    tt(up_t[:, b, :], gate_t[:, b, :], up_t[:, b, :], ALU.mult).then_inc(prod_done, 1)
                    dve.wait_ge(hid_hi_ready, at(l, FT, 1) + f)
                    tt(hid_lo[:, f, :], up_t[:, b, :], hid_hi[:, f, :].bitcast(F32), ALU.subtract)\
                        .then_inc(hid_ready, 1)

                for f in range(4):
                    hidden(f, f % 2, ffn_banks(f))
                with dve.Fori(0, (FT - 4) // 2) as i:
                    for b in range(2):
                        hidden(4 + 2 * i + b, b, ffn_banks(4 + b))
                for t in range(KT):
                    add_square(l, GR_FFN, t)
                rstd(l, GR_FFN)
                residual_and_low(l, KT, GR_FFN, POST_FFN, NEXT_MIX)

            for n in range(2 * ST):
                dve.wait_ge(out_turned, n + 1)
                copy(rows[:, n // 2, (n % 2) * 4 * P:(n % 2 + 1) * 4 * P], bank[n % 2][:, :]).then_inc(out_copied, 1)


_INS = ["x", "pre_mix_g", "w_in", "gmlp_ln_g", "gmlp_ln_b", "gmlp_ws", "gmlp_b", "lambda_q1", "lambda_k1",
        "lambda_q2", "lambda_k2", "subln_g", "w_out", "post_mix_g", "pre_ffn_g", "w_gate_up", "w_down",
        "post_ffn_g"]
_OUTS = [((1, 512, 1024), "float32")]


def rope_table(seq, dim):
    inv = (1.0 / 10000.0 ** (np.arange(0, dim, 2) / dim)).astype(np.float32)
    ang = (np.arange(seq, dtype=np.float32)[:, None] * inv[None, :]).T
    cos, sin = np.cos(ang), np.sin(ang)
    return np.stack([np.concatenate([cos, cos, cos, cos]), np.concatenate([-sin, sin, -sin, sin])]).astype(np.float32)


def kernel(**inputs):
    import concourse.bacc as _bacc
    from concourse.bass_utils import run_bass_kernel_spmd as _run

    nc = _bacc.Bacc("TRN2", target_bir_lowering=False, num_devices=1)
    arrays, args = {}, []
    data = [(name, np.ascontiguousarray(inputs[name])) for name in _INS]
    data.append(("rope", rope_table(inputs["x"].shape[1], inputs["lambda_q1"].shape[1])))
    for name, a in data:
        arrays[f"in_{name}_dram"] = a
        args.append(nc.dram_tensor(f"in_{name}_dram", a.shape, mybir.dt.from_np(a.dtype), kind="ExternalInput").ap())
    for i, (shape, dtype) in enumerate(_OUTS):
        dt = mybir.dt.from_np(np.dtype(dtype))
        args.append(nc.dram_tensor(f"out_{i}_dram", shape, dt, kind="ExternalOutput").ap())
    trunk(nc, *args)
    r = _run(nc, [arrays], core_ids=[0])
    got = tuple(r.results[0][f"out_{i}_dram"] for i in range(len(_OUTS)))
    return got[0]
```

```python
import math
from contextlib import ExitStack

import numpy as np

import concourse.bass as bass
from concourse import mybir

F32 = mybir.dt.float32
F32R = mybir.dt.float32r
ALU = mybir.AluOpType
ACT = mybir.ActivationFunctionType
AX_X = mybir.AxisListType.X

P = 128
EPS = 1e-6
NEG_INF = -1e30


def at(l, n, k):
    return l * n + k


def trunk(nc, x, pre_mix_g, w_in, gmlp_ln_g, gmlp_ln_b, gmlp_ws, gmlp_b, lambda_q1, lambda_k1, lambda_q2,
          lambda_k2, subln_g, w_out, post_mix_g, pre_ffn_g, w_gate_up, w_down, post_ffn_g, rope, out):
    L, D, IN = w_in.shape
    S = x.shape[1]
    FF = w_down.shape[1]
    KT = D // P
    ST = S // P
    G = gmlp_ws.shape[1]
    H = G
    HD = lambda_q1.shape[1]
    CH = 64
    FT = FF // P
    FH = FT // 2
    SCALE = HD ** -0.5
    U0, V0, Q0, K0, A0 = 0, G * P, 2 * G * P, 3 * G * P, 4 * G * P
    assert L == 2 and (S, ST, KT, IN) == (512, 4, 2 * G, 5 * G * P) and 2 * HD == P and FT % 2 == 0

    C_QK, C_VG, C_VA, C_U, C_OUT, C_GU = 0, 4, 6, 8, 10, 14
    C_DOWN = C_GU + FT
    NC = C_DOWN + 2 * KT
    CE = KT * 2 * P
    CD = FH * P
    assert NC % 2 == 0
    QK_TILES = [(K0, 0), (K0, 1), (Q0, 0), (Q0, 1), (K0, 2), (K0, 3), (Q0, 2), (Q0, 3)]
    QK_BANKS = [0, 1, 2, 3, 5, 6, 0, 1]

    POST_MIX, PRE_FFN, POST_FFN, NEXT_MIX, LN_G, LN_B, SUBLN, NEG_LAM = 0, 8, 16, 24, 32, 36, 40, 41
    NPAR = 42
    PAR_ROWS = L * NEG_LAM
    NS = H * ST
    TABLES = 3
    PAR_DMAS = 7 * L
    PAR_STEPS = 1 + 2 * L
    LAM_INIT = [0.8 - 0.6 * math.exp(-0.3 * l) for l in range(L)]

    ctx = ExitStack()
    with ctx:
        def sb(name, shape, dt=F32, stack=ctx):
            return stack.enter_context(nc.sbuf_tensor(name, shape, dt))

        def sem(name):
            return ctx.enter_context(nc.semaphore(name))

        xT = sb("xT", [P, KT, S])
        yT = sb("yT", [P, KT, S])
        with ExitStack() as operand:
            xg_hi = sb("xg_hi", [P, KT, S], F32R, operand)
            xg_lo = sb("xg_lo", [P, KT, S], F32R, operand)
        x_rows = sb("x_rows", [P, ST, D])
        y_rows = sb("y_rows", [P, ST, D])
        raw = sb("raw", [P, 2, CE])
        w_hi = sb("w_hi", [P, 2, 2, CE // 2], F32R)
        w_lo = sb("w_lo", [P, 2, 2, CE // 2], F32R)
        rstd_x = sb("rstd_x", [P, S])
        sq_sum = sb("sq_sum", [P, S])
        diag = sb("diag", [P, ST, P])
        ident = sb("ident", [P, P])
        ones = sb("ones", [P, P])
        par_all = sb("par_all", [P, L, NPAR])
        par = sb("par", [P, NPAR])
        gain0 = sb("gain0", [P, KT])
        eps = sb("eps", [P, 1])
        root = sb("root", [P, ST])
        root_of_one = sb("root_of_one", [P, 1])
        rcol = sb("rcol", [P, 2, ST])
        taken = [0]

        def small(*shape):
            n = math.prod(shape)
            t = sq_sum[:, taken[0]:taken[0] + n]
            taken[0] += n
            names = "abc"[:len(shape)]
            return t.rearrange(f"p ({' '.join(names)}) -> p {' '.join(names)}", **dict(zip(names, shape)))

        mx = small(2)
        nmx = small(2, 2)
        psumr = small(2, 2)
        rinv = small(2)
        w1 = small(1)
        stats = small(ST, 6)
        mv = small(ST, 2)
        ln_root = small(ST)
        ln_rs = small(ST)
        o_mean = small(H, ST)
        o_root = small(H, ST)
        o_rs = small(H, ST)
        with ExitStack() as mixers:
            q_rot = sb("q_rot", [P, H, S], stack=mixers)
            k_rot = sb("k_rot", [P, H, S], stack=mixers)
            swap = sb("swap", [P, 2, S], stack=mixers)
            v_att = sb("v_att", [P, ST, H * P], stack=mixers)
            v_gate = sb("v_gate", [P, ST, G * P], stack=mixers)
            prob = sb("prob", [P, 2, 2, S], stack=mixers)
            attn = sb("attn", [P, 2, S], stack=mixers)
            attnT = sb("attnT", [P, 2, ST, S], stack=mixers)
            o_sq = sb("o_sq", [P, S], stack=mixers)
            trig = sb("trig", [P, 2, S], stack=mixers)
            ws = sb("ws", [P, G, P], stack=mixers)
            wsT = sb("wsT", [P, G, P], stack=mixers)
            g_bias = sb("g_bias", [P, G, P], stack=mixers)
            add_t = sb("add_t", [P, G, P], stack=mixers)
        hid_hi = sb("hid_hi", [P, FT, S], F32R)
        hid_lo = sb("hid_lo", [P, FT, S], F32R)
        oT = yT[:, 0:H, :]
        uT = yT[:, H:H + G, :]
        gate_t = yT[:, 0:2, :]
        up_t = yT[:, 2:4, :]
        rows = attnT[:, :, :, :].rearrange("p a b s -> p (a b s)").rearrange("p (r d) -> p r d", r=ST)
        par_rows = v_att[:, 0, 0:P]
        gain_rows = v_att[:, 1, 0:P]
        lam_in = v_gate[:, 0, 0:4 * L * HD].rearrange("p (v l d) -> p v l d", v=4, l=L)
        lam_prod = v_gate[:, 1, 0:2 * L * HD].rearrange("p (v l d) -> p v l d", v=2, l=L)
        lam_sum = prob[:, 0, 0, 0:2 * L].rearrange("p (v l) -> p v l", v=2)
        lam_exp = prob[:, 0, 1, 0:2 * L].rearrange("p (v l) -> p v l", v=2)
        lam_d = prob[:, 1, 0, 0:L]
        last_sq = diag[:, :, :].rearrange("p r q -> p (r q)")
        o_diag = prob[:, :, :, :].rearrange("p b j s -> p (b j) s").rearrange("p h (r q) -> p h r q", r=ST)

        banks = ctx.enter_context(nc.psum_tensor("banks", [P, 8, 512], F32))
        bank = [banks[:, i, :] for i in range(8)]
        b_tr = [bank[i][:, :].rearrange("p (r q) -> p r q", r=ST) for i in range(8)]
        SQ_BANK, BC_BANK, SSQ_BANK = 5, 4, 7
        X_BANKS = [4, 7, 6]
        T_BANK, WS_BANK, O_BANK = 2, 3, 3
        U_BANKS = [0, 1, 0, 1]
        GATE_BANKS = [0, 0, 0, 1]
        GATE_STEPS = {10: 0, 11: 1, 12: 2, 13: 3}
        OUT_STEPS = {NS: [(0, range(0, 2)), (1, range(0, 2))], NS + 1: [(0, range(2, 4))],
                     NS + 2: [(1, range(2, 4))], NS + 3: [(2, range(0, 2))]}
        OUT_BANKS = [0, 1, 2, 3]
        ssq_col = bank[SSQ_BANK][:, 0:ST]
        ossq_col = bank[O_BANK][:, 0:ST]

        x_landed = [sem(f"x_landed{q}") for q in range(KT // 2)]
        gain0_landed = sem("gain0_landed")
        gain0_turned = sem("gain0_turned")
        gain0_ready = sem("gain0_ready")
        par_landed = sem("par_landed")
        lam_landed = sem("lam_landed")
        consts_ready = sem("consts_ready")
        ident_ready = sem("ident_ready")
        par_turned = sem("par_turned")
        par_ready = sem("par_ready")
        lam_steps = sem("lam_steps")
        lam_ready = sem("lam_ready")
        lam_exp_ready = sem("lam_exp_ready")
        par_loaded = sem("par_loaded")
        x_turned = sem("x_turned")
        w_landed = [sem("w_landed0"), sem("w_landed1")]
        w_hi_ready = sem("w_hi_ready")
        first_low_ready = sem("first_low_ready")
        w_ready = sem("w_ready")
        w_done = sem("w_done")
        x_ready = sem("x_ready")
        xg_hi_ready = sem("xg_hi_ready")
        xg_ready = sem("xg_ready")
        y_sq_ready = sem("y_sq_ready")
        y_sq_summed = sem("y_sq_summed")
        x_sq_ready = sem("x_sq_ready")
        x_sq_summed = sem("x_sq_summed")
        ssq_ready = sem("ssq_ready")
        root_ready = sem("root_ready")
        rcol_ready = sem("rcol_ready")
        diag_ready = sem("diag_ready")
        bc_ready = sem("bc_ready")
        rstd_x_ready = sem("rstd_x_ready")
        tables_landed = sem("tables_landed")
        trig_scaled = sem("trig_scaled")
        qk_swapped = sem("qk_swapped")
        qk_cos = sem("qk_cos")
        qk_sin = sem("qk_sin")
        qk_rotated = sem("qk_rotated")
        vg_gelu = sem("vg_gelu")
        vg_stats = sem("vg_stats")
        vg_var = sem("vg_var")
        ln_root_ready = sem("ln_root_ready")
        ln_rs_ready = sem("ln_rs_ready")
        xhat_ready = sem("xhat_ready")
        va_done = sem("va_done")
        ws_turned = sem("ws_turned")
        ws_copied = sem("ws_copied")
        ws_masked = sem("ws_masked")
        ws_summed = sem("ws_summed")
        add_ready = sem("add_ready")
        u_scaled = sem("u_scaled")
        u_gelu = sem("u_gelu")
        gm_ready = sem("gm_ready")
        gm_added = sem("gm_added")
        ya_mul = sem("ya_mul")
        ya_hi = sem("ya_hi")
        ya_ready = sem("ya_ready")
        sc_ready = sem("sc_ready")
        sc_masked = sem("sc_masked")
        max_ready = sem("max_ready")
        nmax_ready = sem("nmax_ready")
        exp_done = sem("exp_done")
        rinv_ready = sem("rinv_ready")
        w1_ready = sem("w1_ready")
        p1_scaled = sem("p1_scaled")
        a_ready = sem("a_ready")
        at_ready = sem("at_ready")
        at_copied = sem("at_copied")
        pv_ready = sem("pv_ready")
        o_copied = sem("o_copied")
        o_squared = sem("o_squared")
        ossq_ready = sem("ossq_ready")
        o_mean_ready = sem("o_mean_ready")
        o_root_ready = sem("o_root_ready")
        o_rs_ready = sem("o_rs_ready")
        o_diag_ready = sem("o_diag_ready")
        o_bc_ready = sem("o_bc_ready")
        yb_mul = sem("yb_mul")
        yb_hi = sem("yb_hi")
        yb_ready = sem("yb_ready")
        y_copied = sem("y_copied")
        y_scaled = sem("y_scaled")
        g_scaled = sem("g_scaled")
        up_scaled = sem("up_scaled")
        silu_done = sem("silu_done")
        prod_done = sem("prod_done")
        hid_hi_ready = sem("hid_hi_ready")
        hid_ready = sem("hid_ready")
        x_back = sem("x_back")
        y_back = sem("y_back")
        x_back_copied = sem("x_back_copied")
        y_back_copied = sem("y_back_copied")
        out_ready = sem("out_ready")
        out_stored = sem("out_stored")

        def cut(l, c, halves=2):
            return at(l, 2 * NC, 2 * c) + 4 + halves

        def high_cut(l, c, halves=2):
            return at(l, 2 * NC, 2 * c) + halves

        def done(l, c, eighths=8):
            return at(l, 8 * NC, 8 * c) + 16 + eighths

        def landed(l, c, pair=0):
            return at(l, 16 * NC, 32 * (c // 2 + 1)) + 32 * pair

        GR_MIX, GR_X1, GR_FFN, GR_X2 = 1, 2, 3, 4

        w_in_v = w_in.rearrange("l (k p) c -> l p k c", p=P)
        w_out_v = w_out.rearrange("l (k p) c -> l p k c", p=P)
        w_gu_v = w_gate_up.rearrange("l (k p) c -> l p k c", p=P)
        w_dn_v = w_down.rearrange("l (k p) c -> l p k c", p=P)

        def wide(b):
            return raw[:, b, :].rearrange("p (k c) -> p k c", c=4 * P)

        def tall(b):
            return raw[:, b, :].rearrange("p (k c) -> p k c", c=2 * P)

        def down(b):
            return raw[:, b, 0:CD].rearrange("p (k c) -> p k c", c=P)

        def raw_half(kind, b, h):
            if kind == "tall":
                return tall(b)[:, :, h * P:(h + 1) * P]
            if kind == "wide":
                return wide(b)[:, 2 * h:2 * h + 2, :]
            return down(b)

        def part(t, kind, b, h=0):
            if kind == "down":
                return t[:, b, :, :].rearrange("p h e -> p (h e)")[:, 0:CD].rearrange("p (k c) -> p k c", c=P)
            return t[:, b, h, :].rearrange("p (k c) -> p k c", c=P if kind == "tall" else 4 * P)

        def not_last(engine, register, l):
            engine.reg_mov(register, l)
            return engine.If_ne(register, L - 1)

        block = ctx.enter_context(nc.Block())

        @block.sync
        def _(sp):
            x_view = x[0].rearrange("(r p) d -> p r d", p=P)

            def load_x(q):
                d = slice(2 * q * P, (2 * q + 2) * P)
                sp.dma_start(rows[:, :, d], x_view[:, :, d]).then_inc(x_landed[q], 16)

            def load(l, c, b, halves):
                sp.wait_ge(w_ready, cut(l, c - 2))
                for dst, src in halves:
                    sp.dma_start(dst, src).then_inc(w_landed[b], 16)

            def load_wide(l, c, col, k0):
                w = wide(c % 2)
                load(l, c, c % 2, [(w[:, k:k + 2, :], w_in_v[l, :, k0 + k:k0 + k + 2, col:col + 4 * P])
                                   for k in (0, 2)])

            def load_tall(l, c, src, col):
                w = tall(c % 2)
                load(l, c, c % 2, [(w[:, k:k + 4, :], src[:, k:k + 4, col:col + 2 * P]) for k in (4, 0)])

            load_x(0)
            load_tall(0, C_QK, w_in_v[0], K0)
            load_tall(0, C_QK + 1, w_in_v[0], Q0)
            for q in range(1, KT // 2):
                load_x(q)
            n_par = 0
            for layer in range(L):
                base = layer * NEG_LAM
                nxt = min(layer + 1, L - 1)
                for at_row, src, n in ((POST_MIX, post_mix_g[layer], KT), (PRE_FFN, pre_ffn_g[layer], KT),
                                       (POST_FFN, post_ffn_g[layer], KT), (NEXT_MIX, pre_mix_g[nxt], KT),
                                       (LN_G, gmlp_ln_g[layer], G), (LN_B, gmlp_ln_b[layer], G),
                                       (SUBLN, subln_g[layer], 1)):
                    sp.dma_start(par_rows[base + at_row:base + at_row + n, :],
                                  src.rearrange("(k p) -> k p", k=n)).then_inc(par_landed, 16)
                    n_par += 1
            assert n_par == PAR_DMAS
            for n, v in enumerate((lambda_q1, lambda_q2, lambda_k1, lambda_k2)):
                sp.dma_start(lam_in[:, n, :, :], v.partition_broadcast(P)).then_inc(lam_landed, 16)
            sp.wait_ge(first_low_ready, 3)
            with sp.Fori(0, L) as l:
                load_tall(l, C_QK + 2, w_in_v[l], K0 + 2 * P)
                load_tall(l, C_QK + 3, w_in_v[l], Q0 + 2 * P)
                for n in range(2):
                    load_wide(l, C_VG + n, V0, 4 * n)
                for n in range(2):
                    load_wide(l, C_VA + n, A0, 4 * n)
                for n in range(2):
                    load_tall(l, C_U + n, w_in_v[l], U0 + n * 2 * P)
                for n in range(4):
                    load_tall(l, C_OUT + n, w_out_v[l], n * 2 * P)
                with sp.Fori(0, FT // 2) as i:
                    for b in range(2):
                        w = tall(b)
                        load(l, C_GU + 2 * i + b, b,
                             [(w[:, :, j * P:(j + 1) * P],
                               w_gu_v[l, :, :, bass.ds((2 * i + b) * P + j * FF, P)]) for j in (0, 1)])
                with sp.Fori(0, KT) as t:
                    for b in range(2):
                        w = down(b)
                        load(l, C_DOWN + 2 * t + b, b,
                             [(w[:, k:m, :], w_dn_v[l, :, b * FH + k:b * FH + m, bass.ds(t * P, P)])
                              for k, m in ((0, FH // 2), (FH // 2, FH))])
                with sp.register("layer") as layer, not_last(sp, layer, l):
                    load_tall(l, NC, w_in_v[L - 1], K0)
                    load_tall(l, NC + 1, w_in_v[L - 1], Q0)
            for n in range(2 * ST):
                half, r = divmod(n, ST)
                d = slice(half * D // 2, (half + 1) * D // 2)
                sp.wait_ge(out_ready, n + 1)
                sp.dma_start(out[0, r * P:(r + 1) * P, d], x_rows[:, r, d]).then_inc(out_stored, 16)
            sp.wait_ge(out_stored, 16 * 2 * ST)

        @block.gpsimd
        def _(pool):
            nc.gpsimd.memset(ident[:, :], 0.0).then_inc(w_ready, 7)
            pool.wait_ge(w_ready, 7)
            nc.gpsimd.affine_select(out=ident[:, :], in_=ident[:, :], compare_op=ALU.not_equal, fill=1.0, base=0,
                                    pattern=[[-1, P]], channel_multiplier=1).then_inc(ident_ready, 1)

            def low(l, c, b, h, kind):
                pool.wait_ge(w_hi_ready, high_cut(l, c, 2 if kind == "down" else h + 1))
                nc.gpsimd.tensor_tensor(part(w_lo, kind, b, h), raw_half(kind, b, h),
                                        part(w_hi, kind, b, h).bitcast(F32), ALU.subtract)\
                    .then_inc(w_ready, 2 if kind == "down" else 1)

            def low_halves(l, c, b, kind):
                for h in range(2):
                    low(l, c, b, h, kind)

            def sum_x_squares(l, group):
                for k in range(1, KT):
                    pool.wait_ge(x_sq_ready, at(l, 2 * KT, KT * (group // 2) + k + 1))
                    if k == 1:
                        if group:
                            pool.wait_ge(ssq_ready, at(l, 4, group))
                        a = yT[:, 0, :]
                    else:
                        pool.wait_ge(x_sq_summed, at(l, 2 * (KT - 1), (KT - 1) * (group // 2) + k - 1))
                        a = sq_sum[:, :]
                    nc.gpsimd.tensor_tensor(sq_sum[:, :], a, yT[:, k, :], ALU.add).then_inc(x_sq_summed, 1)

            low(0, 1, 1, 1, "tall")
            sum_x_squares(0, 0)
            with pool.Fori(0, L) as l:
                for c in range(C_QK + 2, C_OUT + 1):
                    low_halves(l, c, c % 2, "wide" if C_VG <= c < C_U else "tall")
                low(l, C_OUT + 1, 1, 0, "tall")
                for g in range(G + 1):
                    if g < G:
                        pool.wait_ge(gm_added, at(l, G, g + 1))
                        pool.wait_ge(u_gelu, at(l, G, g + 1))
                        u = uT[:, g, :].rearrange("p (n t) -> p n t", n=ST)
                        nc.gpsimd.tensor_tensor(u, u, v_gate[:, :, g * P:(g + 1) * P], ALU.mult).then_inc(ya_mul, 1)
                    if g:
                        pool.wait_ge(ya_hi, at(l, G, g))
                        nc.gpsimd.tensor_tensor(xg_lo[:, g - 1, :], uT[:, g - 1, :],
                                                xg_hi[:, g - 1, :].bitcast(F32), ALU.subtract).then_inc(ya_ready, 1)
                low(l, C_OUT + 1, 1, 1, "tall")
                for c in range(C_OUT + 2, C_GU + 2):
                    low_halves(l, c, c % 2, "tall")
                sum_x_squares(l, GR_X1)
                for b in range(2):
                    low_halves(l, C_GU + 2 + b, b, "tall")
                with pool.Fori(0, FT // 2 - 2) as i:
                    for b in range(2):
                        low_halves(l, C_GU + 4 + b + 2 * i, b, "tall")
                with pool.Fori(0, KT) as t:
                    for b in range(2):
                        low(l, C_DOWN + b + 2 * t, b, 0, "down")
                with pool.register("layer") as layer, not_last(pool, layer, l):
                    for c in range(2):
                        low_halves(l, NC + c, c, "tall")
                    sum_x_squares(l, GR_X2)

        @block.tensor
        def _(pe):
            mm, tr = nc.tensor.matmul, nc.tensor.transpose

            def product(o, stat, mov, first, last):
                mm(o, stat[0], mov[0], start=first, stop=False)
                mm(o, stat[1], mov[0], start=False, stop=False)
                return mm(o, stat[0], mov[1], start=False, stop=last)

            def xg_pair(k, s=slice(None)):
                return xg_hi[:, k, s], xg_lo[:, k, s]

            def tall_pair(b, k, j):
                return [part(w, "tall", b, j)[:, k, :] for w in (w_hi, w_lo)]

            def pair_of_chunks(l, c, into, tiles_before, between):
                pe.wait_ge(w_ready, cut(l, c + 1, 1))
                for k in range(KT):
                    w = [tall_pair((c + n // 2) % 2, k, n % 2) for n in range(3)]
                    pe.wait_ge(xg_hi_ready, at(l, 2 * KT, tiles_before + k + 1))
                    for n in range(3):
                        mm(bank[into[n]][:, :], w[n][0], xg_hi[:, k, :], start=(k == 0), stop=False)
                        mm(bank[into[n]][:, :], w[n][1], xg_hi[:, k, :], start=False, stop=False)
                    pe.wait_ge(xg_ready, at(l, 2 * KT, tiles_before + k + 1))
                    for n in range(3):
                        last = mm(bank[into[n]][:, :], w[n][0], xg_lo[:, k, :], start=False, stop=(k == KT - 1))
                        if k == KT - 1:
                            last.then_inc(w_done, 4)
                between()
                pe.wait_ge(w_ready, cut(l, c + 1, 2))
                tall_tile((c + 1) % 2, 1, into[3]).then_inc(w_done, 4)

            def tall_tile(b, j, o, ks=range(KT)):
                for k in ks:
                    last = product(bank[o][:, :], tall_pair(b, k, j), xg_pair(k), k == 0, k == KT - 1)
                return last

            def sum_columns(l, group):
                pe.wait_ge(y_sq_summed if group % 2 else x_sq_summed,
                           at(l, 2 * (KT - 1), (KT - 1) * (group // 2 + 1)))
                for r in range(ST):
                    last = mm(ssq_col[:, r:r + 1], sq_sum[:, r * P:(r + 1) * P], ones[:, 0:1],
                              start=(r == 0), stop=(r == ST - 1 and group % 2 == 0))
                if group % 2:
                    pe.wait_ge(y_sq_ready, at(l, 2 * KT, KT * (group // 2 + 1)))
                    for r in range(ST):
                        last = mm(ssq_col[:, r:r + 1], last_sq[:, r * P:(r + 1) * P], ones[:, 0:1],
                                  start=False, stop=(r == ST - 1))
                last.then_inc(ssq_ready, 1)

            def broadcast(l, group):
                for r in range(ST):
                    pe.wait_ge(diag_ready, at(l, 4 * ST, ST * group + r + 1))
                    last = mm(b_tr[BC_BANK][:, r, :], ones[:, :], diag[:, r, :], start=True, stop=True)
                last.then_inc(bc_ready, 1)

            def half_tile(l, c, b, o):
                pe.wait_ge(w_ready, cut(l, c))
                w = [part(t, "down", b) for t in (w_hi, w_lo)]
                for k in range(FH):
                    f = b * FH + k
                    last = product(bank[o][:, :], [v[:, k, :] for v in w], (hid_hi[:, f, :], hid_lo[:, f, :]),
                                   f == 0, f == FT - 1)
                last.then_inc(w_done, 8)

            pe.wait_ge(ident_ready, 1)
            pe.wait_ge(gain0_landed, 16)
            tr(bank[2][:, 0:KT], gain_rows[0:KT, :], ident[0:KT, 0:KT]).then_inc(gain0_turned, 1)
            for k in range(KT):
                if k % 2 == 0:
                    pe.wait_ge(x_landed[k // 2], 16)
                if k >= 3:
                    pe.wait_ge(x_ready, k - 2)
                for r in range(ST):
                    last = tr(b_tr[X_BANKS[k % 3]][:, r, :], rows[:, r, k * P:(k + 1) * P], ident[:, :])
                last.then_inc(x_turned, 1)
            pe.wait_ge(par_landed, 16 * PAR_DMAS)
            tr(bank[5][:, 0:PAR_ROWS], par_rows[0:PAR_ROWS, :], ident[0:PAR_ROWS, 0:PAR_ROWS]).then_inc(par_turned, 1)
            pe.wait_ge(first_low_ready, 3)
            pe.wait_ge(gain0_ready, 1)

            with pe.Fori(0, L) as l:
                pair_of_chunks(l, C_QK, QK_BANKS[0:4], 0, lambda: sum_columns(l, 0))
                broadcast(l, 0)
                for j in range(2):
                    pe.wait_ge(w_ready, cut(l, C_QK + 2, j + 1))
                    tall_tile(0, j, QK_BANKS[4 + j]).then_inc(w_done, 4)
                for j in range(2):
                    pe.wait_ge(w_ready, cut(l, C_QK + 3, j + 1))
                    pe.wait_ge(qk_cos, at(l, 2 * H, j + 1))
                    tall_tile(1, j, QK_BANKS[6 + j]).then_inc(w_done, 4)

                def values(c, into, bank_free):
                    for n in range(4):
                        b, h = n // 2, n % 2
                        pe.wait_ge(w_ready, cut(l, c + b, h + 1))
                        for r in range(ST):
                            if n == 0:
                                bank_free(r)
                            for k in range(2):
                                w = [part(t, "wide", b, h)[:, k, :] for t in (w_hi, w_lo)]
                                last = product(bank[into[r]][:, :],
                                               xg_pair(2 * n + k, slice(r * P, (r + 1) * P)), w,
                                               n == 0 and k == 0, n == 3 and k == 1)
                            if n == 3:
                                last.then_inc(w_done, 1)
                        if n < 3:
                            last.then_inc(w_done, 4)

                def gate_bank_free(r):
                    if r == 0:
                        pe.wait_ge(rstd_x_ready, at(l, 2, 1))
                    elif r < 3:
                        pe.wait_ge(qk_cos, at(l, 2 * H, 4 + r))

                values(C_VG, [4, 5, 6, 7], gate_bank_free)
                values(C_VA, [0, 1, 2, 3], lambda r: pe.wait_ge(qk_cos, at(l, 2 * H, 2 * H)))

                def scores(n):
                    h, i = divmod(n, ST)
                    w = (i + 1) * P
                    if i == 0:
                        pe.wait_ge(qk_rotated, at(l, 2 * H, 4 if h < 2 else 8))
                    if n < 2:
                        pe.wait_ge(vg_gelu, at(l, ST, 2 * n + 2))
                    else:
                        pe.wait_ge(exp_done, at(l, 2 * NS, 2 * (n - 1)))
                    for j in range(2):
                        ps = slice(j * HD, (j + 1) * HD)
                        last = mm(bank[4 + 2 * (n % 2) + j][:, 0:w], q_rot[ps, h, i * P:(i + 1) * P],
                                  k_rot[ps, h, 0:w], start=True, stop=True)
                    last.then_inc(sc_ready, 1)

                def turn(n):
                    i = n % ST
                    pe.wait_ge(a_ready, at(l, NS, n + 1))
                    if n == 0:
                        pe.wait_ge(va_done, at(l, ST, ST))
                    else:
                        pe.wait_ge(at_copied, at(l, NS, n))
                    for k in range(i + 1):
                        last = tr(b_tr[T_BANK][:, k, :], attn[:, n % 2, k * P:(k + 1) * P], ident[:, :])
                    last.then_inc(at_ready, 1)

                def weigh(h):
                    pe.wait_ge(at_copied, at(l, NS, ST * (h + 1)))
                    if h:
                        pe.wait_ge(o_mean_ready, at(l, H, h))
                    else:
                        pe.wait_ge(add_ready, l + 1)
                    for k in range(ST):
                        last = mm(bank[O_BANK][:, k * P:S], v_att[:, k, h * P:(h + 1) * P],
                                  attnT[:, h % 2, k, k * P:S], start=(k == 0), stop=(k == ST - 1))
                    last.then_inc(pv_ready, 1)

                def head_squares(h):
                    pe.wait_ge(o_squared, at(l, H, h + 1))
                    for r in range(ST):
                        last = mm(ossq_col[:, r:r + 1], o_sq[:, r * P:(r + 1) * P], ones[:, 0:1],
                                  start=True, stop=True)
                    last.then_inc(ossq_ready, 1)

                def head_broadcast(h):
                    pe.wait_ge(o_diag_ready, at(l, H, h + 1))
                    mm(bank[4 + h][:, :], ones[:, :], o_diag[:, h, :, :], start=True, stop=True)\
                        .then_inc(o_bc_ready, 1)

                def u_third(n):
                    t, third = divmod(n, 3)
                    if third == 0:
                        pe.wait_ge(w_ready, cut(l, C_U + t // 2, t % 2 + 1))
                        if t == 0:
                            pe.wait_ge(va_done, at(l, ST, 1))
                        elif t >= 2:
                            pe.wait_ge(u_scaled, at(l, G, t - 1))
                    ks = [range(0, 3), range(3, 6), range(6, KT)][third]
                    last = tall_tile(t // 2 % 2, t % 2, U_BANKS[t], ks)
                    if third == 2:
                        last.then_inc(w_done, 4)

                def gate(g):
                    if g == 0:
                        pe.wait_ge(xhat_ready, at(l, ST, ST))
                    if g == 0 or g == 3:
                        pe.wait_ge(u_scaled, at(l, G, 3 if g == 0 else 4))
                    else:
                        pe.wait_ge(gm_added, at(l, G, g))
                    for n in range(ST):
                        last = mm(b_tr[GATE_BANKS[g]][:, n, :], v_gate[:, n, g * P:(g + 1) * P], wsT[:, g, :],
                                  start=True, stop=True)
                    last.then_inc(gm_ready, 1)

                def out_part(n, ks):
                    if ks[0] == 0:
                        pe.wait_ge(w_ready, cut(l, C_OUT + n // 2, n % 2 + 1))
                        if n < 2:
                            pe.wait_ge(gm_added, at(l, G, 3 + n))
                        else:
                            pe.wait_ge(at_copied, at(l, NS, NS))
                    for k in ks:
                        pe.wait_ge(ya_ready, at(l, G, k + 1))
                        product(bank[OUT_BANKS[n]][:, :], tall_pair(n // 2, k, n % 2), xg_pair(k), k == 0, False)

                for n in range(NS + 5):
                    if n < NS:
                        scores(n)
                    if n == 0:
                        pe.wait_ge(tables_landed, at(l, 16 * TABLES, 16 * TABLES))
                        pe.wait_ge(va_done, at(l, ST, 4))
                        for g in range(G):
                            last = tr(b_tr[WS_BANK][:, g, :], ws[:, g, :], ident[:, :])
                        last.then_inc(ws_turned, 1)
                    if n == 2:
                        pe.wait_ge(ws_masked, l + 1)
                        mm(bank[WS_BANK][:, :], ones[:, :], wsT[:, :, :], start=True, stop=True)\
                            .then_inc(ws_summed, 1)
                    if n < 3 * G:
                        u_third(n)
                    if n in GATE_STEPS:
                        gate(GATE_STEPS[n])
                    for tile, ks in OUT_STEPS.get(n, []):
                        out_part(tile, ks)
                    if 2 <= n < NS + 2:
                        turn(n - 2)
                    if n >= 6 and n % ST == 2:
                        weigh((n - 6) // ST)
                    if n >= 8 and n % ST == 0 and n <= NS:
                        head_squares((n - 8) // ST)
                    if n == NS + 3:
                        head_squares(H - 1)
                        for h in range(H - 1):
                            head_broadcast(h)
                        out_part(2, range(2, G))
                        head_broadcast(H - 1)

                for k in range(G, KT):
                    pe.wait_ge(yb_ready, at(l, H, k - G + 1))
                    for n in range(3):
                        last = product(bank[OUT_BANKS[n]][:, :], tall_pair(n // 2, k, n % 2), xg_pair(k),
                                       False, k == KT - 1)
                        if k == KT - 1:
                            last.then_inc(w_done, 4)
                pe.wait_ge(w_ready, cut(l, C_OUT + 1, 2))
                pe.wait_ge(o_mean_ready, at(l, H, H))
                tall_tile(1, 1, OUT_BANKS[3]).then_inc(w_done, 4)
                for n in range(4, KT):
                    pe.wait_ge(w_ready, cut(l, C_OUT + n // 2, n % 2 + 1))
                    pe.wait_ge(y_copied, at(l, 2 * KT, n - 3))
                    tall_tile(n // 2 % 2, n % 2, OUT_BANKS[n - 4]).then_inc(w_done, 4)
                sum_columns(l, GR_MIX)
                broadcast(l, GR_MIX)

                def hidden_tile(c, b, into):
                    for j in range(2):
                        pe.wait_ge(w_ready, cut(l, c, j + 1))
                        tall_tile(b, j, into[j]).then_inc(w_done, 4)

                pair_of_chunks(l, C_GU, [0, 1, 2, 3], KT, lambda: sum_columns(l, GR_X1))
                broadcast(l, GR_X1)
                hidden_tile(C_GU + 2, 0, [5, 6])
                pe.wait_ge(up_scaled, at(l, FT, 1))
                hidden_tile(C_GU + 3, 1, [0, 1])
                with pe.Fori(0, (FT - 4) // 2) as i:
                    pe.wait_ge(up_scaled, at(l, FT, 3) + 2 * i)
                    hidden_tile(C_GU + 4 + 2 * i, 0, [2, 3])
                    pe.wait_ge(up_scaled, at(l, FT, 4) + 2 * i)
                    hidden_tile(C_GU + 5 + 2 * i, 1, [0, 1])

                with pe.register("layer") as layer, not_last(pe, layer, l):
                    with pe.Fori(0, KT // 2) as i:
                        for j in range(2):
                            pe.wait_ge(y_copied, at(l, 2 * KT, KT - 1 + j) + 2 * i)
                            for b in range(2):
                                if j == 0 and b == 0:
                                    pe.wait_ge(up_scaled, at(l, FT, FT - 1))
                                    pe.wait_ge(hid_ready, at(l, FT, FH))
                                if j == 0 and b == 1:
                                    pe.wait_ge(hid_ready, at(l, FT, FT))
                                half_tile(l, C_DOWN + 4 * i + 2 * j + b, b, 2 + j)
                    sum_columns(l, GR_FFN)
                    broadcast(l, GR_FFN)

            l = L - 1

            def turn_back(src, o, ready):
                for r in range(ST):
                    last = tr(b_tr[o][:, r, :], src[:, r * P:(r + 1) * P], ident[:, :])
                last.then_inc(ready, 1)

            def turn_x_back(k):
                if k >= 2:
                    pe.wait_ge(x_back_copied, k - 1)
                turn_back(xT[:, k, :], (0, BC_BANK)[k % 2], x_back)

            def turn_y_back(k):
                pe.wait_ge(y_copied, at(l, 2 * KT, KT + k + 1))
                if k:
                    pe.wait_ge(y_back_copied, k)
                turn_back(yT[:, k, :], 1, y_back)

            for t in range(KT):
                if t == 0:
                    pe.wait_ge(up_scaled, at(l, FT, FT - 1))
                    pe.wait_ge(hid_ready, at(l, FT, FH))
                else:
                    pe.wait_ge(y_copied, at(l, 2 * KT, KT - 1 + t))
                half_tile(l, C_DOWN + 2 * t, 0, 2 + t % 2)
                if t:
                    for k in range(2) if t == 1 else [t]:
                        turn_x_back(k)
                    turn_y_back(t - 1)
                else:
                    pe.wait_ge(hid_ready, at(l, FT, FT))
                    pe.wait_ge(x_ready, at(l, 2 * KT, 2 * KT))
                half_tile(l, C_DOWN + 2 * t + 1, 1, 2 + t % 2)
            sum_columns(l, GR_FFN)
            turn_y_back(KT - 1)

        def ffn_banks(f):
            return (5, 6) if f == 2 else (2, 3) if f == 1 or (f > 2 and f % 2 == 0) else (0, 1)

        @block.scalar
        def _(act):
            fn = nc.scalar.activation

            act.dma_start(gain_rows[0:KT, :], pre_mix_g[0].rearrange("(k p) -> k p", k=KT)).then_inc(gain0_landed, 16)

            def high(l, c, h, b, kind, pair=0):
                act.wait_ge(w_landed[b], landed(l, c, pair))
                act.wait_ge(w_done, done(l, c - 2, 8 if kind == "down" else 4 * h + 4) + 16 * pair)
                fn(part(w_hi, kind, b, h), raw_half(kind, b, h), ACT.Copy)\
                    .then_inc(w_hi_ready, 2 if kind == "down" else 1)

            def gain_and_square(l, tiles_before, k, gain):
                act.wait_ge(x_ready, at(l, 2 * KT, tiles_before + k + 1))
                fn(xg_hi[:, k, :], xT[:, k, :], ACT.Copy, scale=gain).then_inc(xg_hi_ready, 1)
                fn(yT[:, k, :], xT[:, k, :], ACT.Square).then_inc(x_sq_ready, 1)

            def root_of_mean(l, group):
                act.wait_ge(ssq_ready, at(l, 4, group + 1))
                fn(root[:, :], ssq_col, ACT.Sqrt, scale=1.0 / D, bias=eps[:, :]).then_inc(root_ready, 1)

            def copy_rstd_x(l, group):
                act.wait_ge(bc_ready, at(l, 4, group + 1))
                fn(rstd_x[:, :], bank[BC_BANK][:, :], ACT.Copy).then_inc(rstd_x_ready, 1)

            act.wait_ge(consts_ready, 2)
            act.wait_ge(gain0_ready, 1)
            for k in range(KT):
                if k == 2:
                    for c in range(2):
                        for h in range(2):
                            high(0, c, h, c, "tall")
                gain_and_square(0, 0, k, gain0[:, k:k + 1])
            act.wait_ge(lam_ready, 1)
            fn(lam_exp[:, :, :], lam_sum[:, :, :], ACT.Exp).then_inc(lam_exp_ready, 1)

            def root_table():
                fn(root_of_one[:, :], ones[:, 0:1], ACT.Sqrt)

            def output_tile(l, t, group, o, tile_done, gain=1.0):
                act.wait_ge(w_done, tile_done)
                if 2 <= t < KT - 1:
                    act.wait_ge(y_sq_summed, at(l, 2 * (KT - 1), (KT - 1) * (group // 2) + t - 1))
                fn(bank[SQ_BANK + t % 2][:, :] if t < KT - 1 else last_sq, bank[o][:, :], ACT.Square)\
                    .then_inc(y_sq_ready, 1)
                fn(yT[:, t, :], bank[o][:, :], ACT.Copy, scale=gain).then_inc(y_copied, 1)

            with act.Fori(0, L) as l:
                act.wait_ge(w_done, done(l, -1))
                act.dma_start(trig[:, :, :], rope.rearrange("t p s -> p t s")).then_inc(tables_landed, 16)
                act.dma_start(ws[:, :, :], gmlp_ws[l].rearrange("g t s -> t g s")).then_inc(tables_landed, 16)
                act.dma_start(g_bias[:, :, :], gmlp_b[l].partition_broadcast(P)).then_inc(tables_landed, 16)

                root_of_mean(l, 0)
                high(l, C_QK + 2, 0, 0, "tall")
                high(l, C_QK + 2, 1, 0, "tall")
                high(l, C_QK + 3, 0, 1, "tall")
                copy_rstd_x(l, 0)
                high(l, C_QK + 3, 1, 1, "tall")
                for n in range(2 * H):
                    act.wait_ge(w_done, done(l, C_QK + n // 2, 4 * (n % 2) + 4))
                    if n >= 2:
                        act.wait_ge(qk_rotated, at(l, 2 * H, n - 1))
                    q = P // 4
                    for a in range(4):
                        src = a + 1 if a % 2 == 0 else a - 1
                        last = fn(swap[a * q:(a + 1) * q, n % 2, :],
                                  bank[QK_BANKS[n]][src * q:(src + 1) * q, :], ACT.Copy)
                    last.then_inc(qk_swapped, 1)
                    if n >= 4:
                        high(l, C_QK + 2 + n // 2, n % 2, n // 2 % 2, "wide")
                high(l, C_VG + 2, 0, 0, "wide")
                high(l, C_VG + 2, 1, 0, "wide")
                high(l, C_VG + 3, 0, 1, "wide")
                for r in range(ST):
                    act.wait_ge(w_done, done(l, C_VG + 1, 4 + r + 1))
                    fn(v_gate[:, r, :], bank[4 + r][:, :], ACT.Gelu, scale=rcol[:, 0, r:r + 1]).then_inc(vg_gelu, 1)
                high(l, C_VG + 3, 1, 1, "wide")
                high(l, C_VA + 2, 0, 0, "tall")
                high(l, C_VA + 2, 1, 0, "tall")
                high(l, C_VA + 3, 0, 1, "tall")
                for r in range(ST):
                    act.wait_ge(w_done, done(l, C_VA + 1, 4 + r + 1))
                    fn(v_att[:, r, :], bank[r][:, :], ACT.Copy, scale=rcol[:, 0, r:r + 1]).then_inc(va_done, 1)
                high(l, C_VA + 3, 1, 1, "tall")
                act.wait_ge(vg_var, at(l, ST, ST))
                fn(ln_root[:, :], mv[:, :, 1], ACT.Sqrt, bias=eps[:, :]).then_inc(ln_root_ready, 1)

                def exponentials(n):
                    w = (n % ST + 1) * P
                    act.wait_ge(nmax_ready, at(l, NS, n + 1))
                    if n >= 2:
                        act.wait_ge(a_ready, at(l, NS, n - 1))
                    for j in range(2):
                        fn(prob[:, n % 2, j, 0:w], bank[4 + 2 * (n % 2) + j][:, 0:w], ACT.Exp, scale=SCALE,
                           bias=nmx[:, n % 2, j:j + 1], accum_out=psumr[:, n % 2, j:j + 1]).then_inc(exp_done, 1)

                def copy_turned(n):
                    h, i = divmod(n, ST)
                    act.wait_ge(at_ready, at(l, NS, n + 1))
                    if h >= 2 and i == 0:
                        act.wait_ge(pv_ready, at(l, H, h - 1))
                    fn(attnT[:, h % 2, 0:i + 1, i * P:(i + 1) * P], b_tr[T_BANK][:, 0:i + 1, :], ACT.Copy)\
                        .then_inc(at_copied, 1)

                def copy_head(h):
                    act.wait_ge(pv_ready, at(l, H, h + 1))
                    fn(oT[:, h, :], bank[O_BANK][:, :], ACT.Copy).then_inc(o_copied, 1)
                    if h:
                        act.wait_ge(ossq_ready, at(l, H, h))
                    fn(o_sq[:, :], bank[O_BANK][:, :], ACT.Square).then_inc(o_squared, 1)

                def mean_of_head(h):
                    act.wait_ge(ossq_ready, at(l, H, h + 1))
                    fn(o_mean[:, h, :], ossq_col, ACT.Copy, scale=1.0 / P).then_inc(o_mean_ready, 1)

                def head_roots(n, lo, hi):
                    act.wait_ge(o_mean_ready, at(l, H, hi))
                    fn(o_root[:, lo:hi, :], o_mean[:, lo:hi, :], ACT.Sqrt, bias=eps[:, :]).then_inc(o_root_ready, 1)

                def gated_high(g):
                    act.wait_ge(ya_mul, at(l, G, g + 1))
                    fn(xg_hi[:, g, :], uT[:, g, :], ACT.Copy).then_inc(ya_hi, 1)

                def head_high(h):
                    act.wait_ge(yb_mul, at(l, H, h + 1))
                    fn(xg_hi[:, G + h, :], oT[:, h, :], ACT.Copy).then_inc(yb_hi, 1)

                for n in range(NS + 2):
                    if n == 3 * G + 2:
                        gated_high(1)
                    if n == 3 * G + 3:
                        gated_high(2)
                        gated_high(3)
                    if n < NS:
                        exponentials(n)
                    if n == 0:
                        act.wait_ge(ws_turned, l + 1)
                        fn(wsT[:, :, :], b_tr[WS_BANK][:, :, :], ACT.Copy).then_inc(ws_copied, 1)
                    if 2 <= n and n != 3 * G + 1:
                        copy_turned(n - 2)
                    if n and n % 3 == 0 and n < 3 * G:
                        t = n // 3 - 1
                        high(l, C_U + 2 + t // 2, t % 2, t // 2, "tall")
                    if n == 3 * G:
                        for g in range(G):
                            if g == 1:
                                copy_turned(n - 1)
                            act.wait_ge(u_scaled, at(l, G, g + 1))
                            fn(uT[:, g, :], uT[:, g, :], ACT.Gelu).then_inc(u_gelu, 1)
                    if n == 3 * G + 1:
                        gated_high(0)
                        high(l, C_OUT + 1, 1, 1, "tall")
                    if n >= 6 and n % ST == 2:
                        copy_head((n - 6) // ST)
                    if n >= 8 and n % ST == 0:
                        mean_of_head((n - 8) // ST)
                head_roots(0, 0, H - 1)
                copy_head(H - 1)
                mean_of_head(H - 1)
                head_roots(1, H - 1, H)
                for h in range(H):
                    head_high(h)

                for t in range(KT):
                    if t < KT - 1:
                        high(l, C_OUT + 2 + t // 2, t % 2, t // 2 % 2, "tall")
                    else:
                        root_table()
                    output_tile(l, t, GR_MIX, OUT_BANKS[t % 4], done(l, C_OUT + t // 2, 4 * (t % 2) + 4))
                root_of_mean(l, GR_MIX)
                high(l, C_GU + 1, 1, 1, "tall")
                for k in range(KT):
                    gain_and_square(l, KT, k, par[:, PRE_FFN + k:PRE_FFN + k + 1])
                root_of_mean(l, GR_X1)
                high(l, C_GU + 2, 0, 0, "tall")
                high(l, C_GU + 2, 1, 0, "tall")
                high(l, C_GU + 3, 0, 1, "tall")
                copy_rstd_x(l, GR_X1)
                high(l, C_GU + 3, 1, 1, "tall")

                def hidden(f, b):
                    act.wait_ge(g_scaled, at(l, FT, 1) + f)
                    fn(gate_t[:, b, :], gate_t[:, b, :], ACT.Silu).then_inc(silu_done, 1)
                    act.wait_ge(prod_done, at(l, FT, 1) + f)
                    fn(hid_hi[:, f, :], up_t[:, b, :], ACT.Copy).then_inc(hid_hi_ready, 1)

                hidden(0, 0)
                hidden(1, 1)
                with act.Fori(0, (FT - 4) // 2) as i:
                    for b in range(2):
                        high(l, C_GU + 4 + b, 0, b, "tall", i)
                        high(l, C_GU + 4 + b, 1, b, "tall", i)
                        hidden(2 * i + 2 + b, b)
                for b in range(2):
                    high(l, C_DOWN + b, 0, b, "down")
                    hidden(FT - 2 + b, b)
                with act.register("layer") as layer, not_last(act, layer, l):
                    for c in range(2 * KT):
                        if c < 2 * KT - 2:
                            high(l, C_DOWN + 2 + c, 0, c % 2, "down")
                        elif c == 2 * KT - 2:
                            for h in range(2):
                                high(l, NC, h, 0, "tall")
                        else:
                            root_table()
                        if c % 2:
                            output_tile(l, c // 2, GR_FFN, 2 + c // 2 % 2, done(l, C_DOWN + c))
                    root_of_mean(l, GR_FFN)
                    for h in range(2):
                        high(l, NC + 1, h, 1, "tall")
                    for k in range(KT):
                        gain_and_square(l, 2 * KT, k, par[:, NEXT_MIX + k:NEXT_MIX + k + 1])

            l = L - 1
            for c in range(2 * KT):
                if c < 2 * KT - 2:
                    high(l, C_DOWN + 2 + c, 0, c % 2, "down")
                elif c == 2 * KT - 1:
                    root_table()
                if c % 2:
                    output_tile(l, c // 2, GR_FFN, 2 + c // 2 % 2, done(l, C_DOWN + c),
                                par[:, POST_FFN + c // 2:POST_FFN + c // 2 + 1])
            root_of_mean(l, GR_FFN)

        @block.vector
        def _(dve):
            tt, ts, stt, copy = (nc.vector.tensor_tensor, nc.vector.tensor_scalar, nc.vector.scalar_tensor_tensor,
                                 nc.vector.tensor_copy)
            nc.vector.memset(ones[:, :], 1.0).then_inc(w_done, 16)
            nc.vector.memset(eps[:, :], EPS).then_inc(consts_ready, 2)

            dve.wait_ge(gain0_turned, 1)
            copy(gain0[:, :], bank[2][:, 0:KT]).then_inc(gain0_ready, 1)

            def low_part(l, tiles_before, k, gain):
                dve.wait_ge(xg_hi_ready, at(l, 2 * KT, tiles_before + k + 1))
                stt(xg_lo[:, k, :], xT[:, k, :], gain, xg_hi[:, k, :].bitcast(F32), ALU.mult, ALU.subtract)\
                    .then_inc(xg_ready, 1)

            def sum_y_squares(l, group, behind=lambda k: None):
                for k in range(KT - 1):
                    if k:
                        behind(k)
                    dve.wait_ge(y_sq_ready, at(l, 2 * KT, KT * (group // 2) + k + 1))
                    if k == 0:
                        dve.wait_ge(ssq_ready, at(l, 4, group))
                        copy(sq_sum[:, :], bank[SQ_BANK][:, :]).then_inc(y_sq_summed, 1)
                    else:
                        dve.wait_ge(y_sq_summed, at(l, 2 * (KT - 1), (KT - 1) * (group // 2) + k))
                        tt(sq_sum[:, :], bank[SQ_BANK + k % 2][:, :], sq_sum[:, :], ALU.add)\
                            .then_inc(y_sq_summed, 1)

            def rstd(l, group):
                c = rcol[:, group % 2, :]
                dve.wait_ge(root_ready, at(l, 4, group + 1))
                nc.vector.reciprocal(c, root[:, :]).then_inc(rcol_ready, 1)
                dve.wait_ge(rcol_ready, at(l, 4, group + 1))
                for r in range(ST):
                    ts(diag[:, r, :], ident[:, :], c[:, r:r + 1], None, ALU.mult).then_inc(diag_ready, 1)

            def scale_y(l, tiles_before, k, gain):
                stt(yT[:, k, :], yT[:, k, :], gain, bank[BC_BANK][:, :], ALU.mult, ALU.mult).then_inc(y_scaled, 1)

            def residual(l, tiles_before, k):
                dve.wait_ge(y_scaled, at(l, 2 * KT, tiles_before + k + 1))
                tt(xT[:, k, :], xT[:, k, :], yT[:, k, :], ALU.add).then_inc(x_ready, 1)

            def residual_and_low(l, tiles_before, group, gain_y, gain_x):
                dve.wait_ge(bc_ready, at(l, 4, group + 1))
                dve.wait_ge(y_copied, at(l, 2 * KT, tiles_before + KT))
                for k in range(KT + 1):
                    if k < KT:
                        scale_y(l, tiles_before, k, par[:, gain_y + k:gain_y + k + 1])
                    if k:
                        low_part(l, tiles_before + KT, k - 1, par[:, gain_x + k - 1:gain_x + k])
                    if k < KT:
                        residual(l, tiles_before, k)

            dve.wait_ge(ident_ready, 1)

            def take_x(k):
                dve.wait_ge(x_turned, k + 1)
                copy(xT[:, k, :], bank[X_BANKS[k % 3]][:, :]).then_inc(x_ready, 1)

            def first_low(c, h):
                dve.wait_ge(w_hi_ready, high_cut(0, c, h + 1))
                tt(part(w_lo, "tall", c, h), raw_half("tall", c, h), part(w_hi, "tall", c, h).bitcast(F32),
                   ALU.subtract).then_inc(first_low_ready, 1)

            for k in range(2):
                take_x(k)
            for k in range(2):
                low_part(0, 0, k, gain0[:, k:k + 1])
            first_low(0, 0)
            first_low(0, 1)
            for k in range(2, 4):
                take_x(k)
            first_low(1, 0)
            take_x(4)
            low_part(0, 0, 2, gain0[:, 2:3])
            for k in range(5, KT):
                take_x(k)
            for k in range(3, KT):
                low_part(0, 0, k, gain0[:, k:k + 1])
            dve.wait_ge(par_turned, 1)
            copy(par_all[:, :, 0:NEG_LAM], bank[5][:, 0:L * NEG_LAM].rearrange("p (l n) -> p l n", l=L))\
                .then_inc(par_ready, 1)
            dve.wait_ge(lam_landed, 16 * 4)
            tt(lam_prod, lam_in[:, 0:2, :, :], lam_in[:, 2:4, :, :], ALU.mult).then_inc(lam_steps, 1)
            dve.wait_ge(lam_steps, 1)
            nc.vector.tensor_reduce(lam_sum[:, :, :], lam_prod, AX_X, ALU.add).then_inc(lam_ready, 1)
            dve.wait_ge(lam_exp_ready, 1)
            tt(lam_d[:, :], lam_exp[:, 1, :], lam_exp[:, 0, :], ALU.subtract).then_inc(lam_steps, 1)
            dve.wait_ge(lam_steps, 2)
            dve.wait_ge(par_ready, 1)
            for l in range(L):
                ts(par_all[:, l, NEG_LAM:NEG_LAM + 1], lam_d[:, l:l + 1], -LAM_INIT[l], None, ALU.add)\
                    .then_inc(par_ready, 1)
                ts(par_all[:, l, SUBLN:SUBLN + 1], par_all[:, l, SUBLN:SUBLN + 1], 1.0 - LAM_INIT[l], None, ALU.mult)\
                    .then_inc(par_ready, 1)
            dve.wait_ge(par_ready, PAR_STEPS)

            with dve.Fori(0, L) as l:
                dve.wait_ge(xg_ready, at(l, 2 * KT, KT))
                copy(par[:, :], par_all[:, l, :]).then_inc(par_loaded, 1)
                dve.wait_ge(par_loaded, l + 1)
                rstd(l, 0)
                dve.wait_ge(tables_landed, at(l, 16 * TABLES, 16 * TABLES))
                dve.wait_ge(rstd_x_ready, at(l, 2, 1))
                tt(trig[:, :, :], trig[:, :, :], rstd_x[:, :].unsqueeze(1).to_broadcast([P, 2, S]), ALU.mult)\
                    .then_inc(trig_scaled, 1)
                dve.wait_ge(trig_scaled, l + 1)
                for n, (col, h) in enumerate(QK_TILES):
                    dst = (k_rot if col == K0 else q_rot)[:, h, :]
                    dve.wait_ge(qk_swapped, at(l, 2 * H, n + 1))
                    tt(dst, bank[QK_BANKS[n]][:, :], trig[:, 0, :], ALU.mult).then_inc(qk_cos, 1)
                    tt(swap[:, n % 2, :], swap[:, n % 2, :], trig[:, 1, :], ALU.mult).then_inc(qk_sin, 1)
                    dve.wait_ge(qk_cos, at(l, 2 * H, n + 1))
                    dve.wait_ge(qk_sin, at(l, 2 * H, n + 1))
                    tt(dst, dst, swap[:, n % 2, :], ALU.add).then_inc(qk_rotated, 1)
                for r in range(ST):
                    dve.wait_ge(vg_gelu, at(l, ST, r + 1))
                    nc.vector.bn_stats(stats[:, r, :], v_gate[:, r, :]).then_inc(vg_stats, 1)
                dve.wait_ge(vg_stats, at(l, ST, ST))

                def maxima(n):
                    b, w, i = 4 + 2 * (n % 2), (n % ST + 1) * P, n % ST
                    dve.wait_ge(sc_ready, at(l, NS, n + 1))
                    nc.vector.memset(banks[0:CH, b:b + 2, w - CH:w], NEG_INF).then_inc(sc_masked, 1)
                    dve.wait_ge(sc_masked, at(l, NS, n + 1))
                    nc.vector.tensor_reduce(mx[:, :], banks[:, b:b + 2, 0:w], AX_X, ALU.max).then_inc(max_ready, 1)
                    dve.wait_ge(max_ready, at(l, NS, n + 1))
                    ts(nmx[:, n % 2, :], mx[:, :], -SCALE, None, ALU.mult).then_inc(nmax_ready, 1)

                def combine(n):
                    b, w = n % 2, (n % ST + 1) * P
                    dve.wait_ge(exp_done, at(l, 2 * NS, 2 * n + 2))
                    if n == 3 * G + 2:
                        dve.wait_ge(a_ready, at(l, NS, n))
                    nc.vector.reciprocal(rinv[:, :], psumr[:, b, :]).then_inc(rinv_ready, 1)
                    dve.wait_ge(rinv_ready, at(l, NS, n + 1))
                    tt(w1[:, :], rinv[:, 1:2], par[:, NEG_LAM:NEG_LAM + 1], ALU.mult).then_inc(w1_ready, 1)
                    dve.wait_ge(w1_ready, at(l, NS, n + 1))
                    ts(prob[:, b, 1, 0:w], prob[:, b, 1, 0:w], w1[:, :], None, ALU.mult).then_inc(p1_scaled, 1)
                    dve.wait_ge(p1_scaled, at(l, NS, n + 1))
                    if n >= 2:
                        dve.wait_ge(at_ready, at(l, NS, n - 1))
                    stt(attn[:, b, 0:w], prob[:, b, 0, 0:w], rinv[:, 0:1], prob[:, b, 1, 0:w], ALU.mult, ALU.add)\
                        .then_inc(a_ready, 1)

                def normalize_gate(r):
                    if r == 0:
                        dve.wait_ge(ln_root_ready, l + 1)
                        nc.vector.reciprocal(ln_rs[:, :], ln_root[:, :]).then_inc(ln_rs_ready, 1)
                        dve.wait_ge(ln_rs_ready, l + 1)
                    ts(v_gate[:, r, :], v_gate[:, r, :], mv[:, r, 0:1], ln_rs[:, r:r + 1], ALU.subtract, ALU.mult)\
                        .then_inc(xhat_ready, 1)

                def additive_terms():
                    dve.wait_ge(ws_summed, l + 1)
                    for g in range(G):
                        last = stt(add_t[:, g, :], b_tr[WS_BANK][:, g, :], par[:, LN_B + g:LN_B + g + 1],
                                   g_bias[:, g, :], ALU.mult, ALU.add)
                    last.then_inc(add_ready, 1)

                def scale_u(t):
                    dve.wait_ge(w_done, done(l, C_U + t // 2, 4 * (t % 2) + 4))
                    tt(uT[:, t, :], bank[U_BANKS[t]][:, :], rstd_x[:, :], ALU.mult).then_inc(u_scaled, 1)

                def add_terms(g):
                    dve.wait_ge(gm_ready, at(l, G, g + 1))
                    dve.wait_ge(add_ready, l + 1)
                    stt(v_gate[:, :, g * P:(g + 1) * P], b_tr[GATE_BANKS[g]][:, :, :], par[:, LN_G + g:LN_G + g + 1],
                        add_t[:, g, :].unsqueeze(1).to_broadcast([P, ST, P]), ALU.mult, ALU.add).then_inc(gm_added, 1)

                def head_rs(n, lo, hi):
                    dve.wait_ge(o_root_ready, at(l, 2, n + 1))
                    nc.vector.reciprocal(o_rs[:, lo:hi, :], o_root[:, lo:hi, :]).then_inc(o_rs_ready, 1)
                    dve.wait_ge(o_rs_ready, at(l, 2, n + 1))

                def head_diag(h):
                    tt(o_diag[:, h, :, :], ident[:, :].unsqueeze(1).to_broadcast([P, ST, P]),
                       o_rs[:, h, :].unsqueeze(2).to_broadcast([P, ST, P]), ALU.mult).then_inc(o_diag_ready, 1)

                def head_scale(h):
                    dve.wait_ge(o_copied, at(l, H, h + 1))
                    dve.wait_ge(o_bc_ready, at(l, H, h + 1))
                    stt(oT[:, h, :], oT[:, h, :], par[:, SUBLN:SUBLN + 1], bank[4 + h][:, :], ALU.mult, ALU.mult)\
                        .then_inc(yb_mul, 1)

                def head_low(h):
                    dve.wait_ge(yb_hi, at(l, H, h + 1))
                    tt(xg_lo[:, G + h, :], oT[:, h, :], xg_hi[:, G + h, :].bitcast(F32), ALU.subtract)\
                        .then_inc(yb_ready, 1)

                for n in range(NS + 1):
                    if n and n % 3 == 0 and n <= 3 * G:
                        scale_u(n // 3 - 1)
                    if n - 1 in GATE_STEPS:
                        add_terms(GATE_STEPS[n - 1])
                    if n == 1:
                        dve.wait_ge(ws_copied, l + 1)
                        nc.vector.memset(wsT[CH:P, :, 0:CH], 0.0).then_inc(ws_masked, 1)
                    early = n == 3 * G + 2
                    if early:
                        maxima(n)
                    if n:
                        combine(n - 1)
                    if n < NS and not early:
                        maxima(n)
                    if n == 0:
                        for r in range(ST):
                            nc.vector.bn_aggr(mv[:, r, :], stats[:, r, :]).then_inc(vg_var, 1)
                    if n in (1, 2, 4, 5):
                        normalize_gate((1, 2, 4, 5).index(n))
                    if n == 4:
                        additive_terms()
                head_rs(0, 0, H - 1)
                head_diag(0)
                head_diag(1)
                head_diag(2)
                head_rs(1, H - 1, H)
                head_diag(3)
                head_scale(0)
                head_scale(1)
                head_low(0)
                head_scale(2)
                head_low(1)
                head_scale(3)
                head_low(2)
                head_low(3)

                sum_y_squares(l, GR_MIX)
                rstd(l, GR_MIX)
                residual_and_low(l, 0, GR_MIX, POST_MIX, PRE_FFN)
                rstd(l, GR_X1)
                dve.wait_ge(rstd_x_ready, at(l, 2, 2))

                def hidden(f, b, into):
                    dve.wait_ge(w_done, done(l, C_GU) + 8 * f)
                    tt(gate_t[:, b, :], bank[into[0]][:, :], rstd_x[:, :], ALU.mult).then_inc(g_scaled, 1)
                    tt(up_t[:, b, :], bank[into[1]][:, :], rstd_x[:, :], ALU.mult).then_inc(up_scaled, 1)
                    dve.wait_ge(silu_done, at(l, FT, 1) + f)
                    dve.wait_ge(up_scaled, at(l, FT, 1) + f)
                    tt(up_t[:, b, :], gate_t[:, b, :], up_t[:, b, :], ALU.mult).then_inc(prod_done, 1)
                    dve.wait_ge(hid_hi_ready, at(l, FT, 1) + f)
                    tt(hid_lo[:, f, :], up_t[:, b, :], hid_hi[:, f, :].bitcast(F32), ALU.subtract)\
                        .then_inc(hid_ready, 1)

                for f in range(4):
                    hidden(f, f % 2, ffn_banks(f))
                with dve.Fori(0, (FT - 4) // 2) as i:
                    for b in range(2):
                        hidden(4 + 2 * i + b, b, ffn_banks(4 + b))
                with dve.register("layer") as layer, not_last(dve, layer, l):
                    sum_y_squares(l, GR_FFN)
                    rstd(l, GR_FFN)
                    residual_and_low(l, KT, GR_FFN, POST_FFN, NEXT_MIX)

            l = L - 1

            def copy_back(k, from_bank, to, turned, copied):
                dve.wait_ge(turned, k + 1)
                if k == 0:
                    dve.wait_ge(w_done, done(l, C_DOWN - 1))
                copy(to[:, :, k * P:(k + 1) * P], b_tr[from_bank][:, :, :]).then_inc(copied, 1)

            def copy_back_tiles(t):
                for k in range(2) if t == 1 else [t]:
                    copy_back(k, (0, BC_BANK)[k % 2], x_rows, x_back, x_back_copied)
                copy_back(t - 1, 1, y_rows, y_back, y_back_copied)

            sum_y_squares(l, GR_FFN, copy_back_tiles)
            copy_back_tiles(KT - 1)
            copy_back(KT - 1, 1, y_rows, y_back, y_back_copied)
            dve.wait_ge(root_ready, at(l, 4, GR_FFN + 1))
            nc.vector.reciprocal(rcol[:, 1, :], root[:, :]).then_inc(rcol_ready, 1)
            dve.wait_ge(rcol_ready, at(l, 4, GR_FFN + 1))
            dve.wait_ge(x_back_copied, KT)
            dve.wait_ge(y_back_copied, KT)
            for n in range(2 * ST):
                half, r = divmod(n, ST)
                d = slice(half * D // 2, (half + 1) * D // 2)
                stt(x_rows[:, r, d], y_rows[:, r, d], rcol[:, 1, r:r + 1], x_rows[:, r, d], ALU.mult, ALU.add)\
                    .then_inc(out_ready, 1)


_INS = ["x", "pre_mix_g", "w_in", "gmlp_ln_g", "gmlp_ln_b", "gmlp_ws", "gmlp_b", "lambda_q1", "lambda_k1",
        "lambda_q2", "lambda_k2", "subln_g", "w_out", "post_mix_g", "pre_ffn_g", "w_gate_up", "w_down",
        "post_ffn_g"]
_OUTS = [((1, 512, 1024), "float32")]


def rope_table(seq, dim):
    inv = (1.0 / 10000.0 ** (np.arange(0, dim, 2) / dim)).astype(np.float32)
    ang = (np.arange(seq, dtype=np.float32)[:, None] * inv[None, :]).T
    cos, sin = np.cos(ang), np.sin(ang)
    return np.stack([np.concatenate([cos, cos, cos, cos]), np.concatenate([-sin, sin, -sin, sin])]).astype(np.float32)


def kernel(**inputs):
    import concourse.bacc as _bacc
    from concourse.bass_utils import run_bass_kernel_spmd as _run

    nc = _bacc.Bacc("TRN2", target_bir_lowering=False, num_devices=1)
    arrays, args = {}, []
    data = [(name, np.ascontiguousarray(inputs[name])) for name in _INS]
    data.append(("rope", rope_table(inputs["x"].shape[1], inputs["lambda_q1"].shape[1])))
    for name, a in data:
        arrays[f"in_{name}_dram"] = a
        args.append(nc.dram_tensor(f"in_{name}_dram", a.shape, mybir.dt.from_np(a.dtype), kind="ExternalInput").ap())
    for i, (shape, dtype) in enumerate(_OUTS):
        dt = mybir.dt.from_np(np.dtype(dtype))
        args.append(nc.dram_tensor(f"out_{i}_dram", shape, dt, kind="ExternalOutput").ap())
    trunk(nc, *args)
    r = _run(nc, [arrays], core_ids=[0])
    got = tuple(r.results[0][f"out_{i}_dram"] for i in range(len(_OUTS)))
    return got[0]
```
